# Optimizing a Trainium2 kernel written in Bass

```python
import math
import jax, jax.numpy as jnp
from jax import lax
import numpy as np

D_MODEL = 2048
BATCH = 1
SEQ = 256
DEPTH = 2

N_EVEN = (DEPTH + 1) // 2
N_ODD = DEPTH // 2
EPS = 1e-6
ROPE_THETA = 10000.0
Q_BLOCK = 128
A_HEADS = 8
A_HALF_DIM = 64
A_V_DIM = 2 * A_HALF_DIM
A_WIDTH = A_HEADS * A_V_DIM
B_HEADS = 8
B_HEAD_DIM = 128
B_WIDTH = B_HEADS * B_HEAD_DIM
AB_IN = 3 * A_WIDTH + 3 * B_WIDTH
AB_OUT = A_WIDTH + B_WIDTH
C_Q_HEADS = 32
C_KV_HEADS = 4
C_HEAD_DIM = 64
WINDOW = 128
C_KV_WIDTH = C_KV_HEADS * C_HEAD_DIM
C_OUT = C_Q_HEADS * C_HEAD_DIM
C_IN = C_OUT + 2 * C_KV_WIDTH
D_FF = 4 * D_MODEL

kernel_name = 'hybrid_diffattn_stickbreak_swa_sink_trunk'

def rms_norm(x, g):
    xf = x.astype(jnp.float32)
    y = xf * lax.rsqrt(jnp.mean(xf * xf, axis=-1, keepdims=True) + EPS)
    return (y * g.astype(jnp.float32)).astype(x.dtype)

def rope(x, positions):
    d = x.shape[-1]
    inv_freq = ROPE_THETA ** (-jnp.arange(0, d, 2, dtype=jnp.float32) / d)
    ang = positions.astype(jnp.float32)[..., None] * inv_freq
    cos = jnp.cos(ang)[:, :, None, :]
    sin = jnp.sin(ang)[:, :, None, :]
    xf = x.astype(jnp.float32)
    x1, x2 = xf[..., : d // 2], xf[..., d // 2:]
    out = jnp.concatenate([x1 * cos - x2 * sin, x2 * cos + x1 * sin], axis=-1)
    return out.astype(x.dtype)

def lambda_init_fn(layer):
    return 0.8 - 0.6 * math.exp(-0.3 * layer)

def differential_attention(q1, q2, k1, k2, v, lam):
    B, S, H, dh = q1.shape
    nb = S // Q_BLOCK
    scale = dh ** -0.5
    qs = jnp.stack([q1, q2], axis=2)
    ks = jnp.stack([k1, k2], axis=2)
    qblocks = jnp.moveaxis(qs.reshape(B, nb, Q_BLOCK, 2, H, dh), 1, 0)
    kpos = jnp.arange(S)

    def block(args):
        qblk, i = args
        qpos = i * Q_BLOCK + jnp.arange(Q_BLOCK)
        s = jnp.einsum('bqmhd,bkmhd->bmhqk', qblk, ks).astype(jnp.float32) * scale
        causal = kpos[None, :] <= qpos[:, None]
        s = jnp.where(causal, s, -jnp.inf)
        p = jax.nn.softmax(s, axis=-1)
        p = p[:, 0] - lam * p[:, 1]
        return jnp.einsum('bhqk,bkhe->bqhe', p.astype(v.dtype), v)

    o = lax.map(block, (qblocks, jnp.arange(nb)))
    return jnp.moveaxis(o, 0, 1).reshape(B, S, H, 2 * dh)

def stick_breaking_attention(q, k, v):
    B, S, H, d = q.shape
    nb = S // Q_BLOCK
    scale = d ** -0.5
    qblocks = jnp.moveaxis(q.reshape(B, nb, Q_BLOCK, H, d), 1, 0)
    kpos = jnp.arange(S)

    def block(args):
        qblk, i = args
        qpos = i * Q_BLOCK + jnp.arange(Q_BLOCK)
        z = jnp.einsum('bqhd,bkhd->bhqk', qblk, k).astype(jnp.float32) * scale
        strict = kpos[None, :] < qpos[:, None]
        log1m_beta = jnp.where(strict, jax.nn.log_sigmoid(-z), 0.0)
        after = lax.cumsum(log1m_beta, axis=3, reverse=True) - log1m_beta
        w = jnp.where(strict, jnp.exp(jax.nn.log_sigmoid(z) + after), 0.0)
        return jnp.einsum('bhqk,bkhd->bqhd', w.astype(v.dtype), v)

    o = lax.map(block, (qblocks, jnp.arange(nb)))
    return jnp.moveaxis(o, 0, 1).reshape(B, S, H, d)

def sliding_window_sink_attention(q, k, v, sinks):
    B, S, HQ, dh = q.shape
    HKV = k.shape[2]
    G = HQ // HKV
    nb = S // WINDOW
    scale = dh ** -0.5
    qb = q.reshape(B, nb, WINDOW, HKV, G, dh)
    kb = k.reshape(B, nb, WINDOW, HKV, dh)
    vb = v.reshape(B, nb, WINDOW, HKV, dh)
    pad = ((0, 0), (1, 0), (0, 0), (0, 0), (0, 0))
    kband = jnp.concatenate([jnp.pad(kb, pad)[:, :-1], kb], axis=2)
    vband = jnp.concatenate([jnp.pad(vb, pad)[:, :-1], vb], axis=2)
    s = jnp.einsum('bnqhgd,bnkhd->bnhgqk', qb, kband).astype(jnp.float32) * scale
    qi = jnp.arange(WINDOW)[:, None]
    ki = jnp.arange(2 * WINDOW)[None, :]
    dist = qi + WINDOW - ki
    in_window = (dist >= 0) & (dist < WINDOW)
    real_key = (jnp.arange(nb)[:, None, None] > 0) | (ki[None] >= WINDOW)
    mask = in_window[None] & real_key
    s = jnp.where(mask[None, :, None, None], s, -jnp.inf)
    sink = jnp.broadcast_to(sinks.astype(jnp.float32).reshape(1, 1, HKV, G, 1, 1),
                            s.shape[:-1] + (1,))
    p = jax.nn.softmax(jnp.concatenate([s, sink], axis=-1), axis=-1)[..., :-1]
    o = jnp.einsum('bnhgqk,bnkhd->bnqhgd', p.astype(v.dtype), vband)
    return o.reshape(B, S, HQ, dh)

def even_mixer(h, positions, w_in, w_out, lq1, lk1, lq2, lk2, subln, layer):
    B, S, _ = h.shape
    proj = h @ w_in
    splits = [A_WIDTH, 2 * A_WIDTH, 3 * A_WIDTH, 3 * A_WIDTH + B_WIDTH, 3 * A_WIDTH + 2 * B_WIDTH]
    qa, ka, va, qs, ks, vs = jnp.split(proj, splits, axis=-1)
    qa = qa.reshape(B, S, A_HEADS, 2, A_HALF_DIM)
    ka = ka.reshape(B, S, A_HEADS, 2, A_HALF_DIM)
    q1, q2 = rope(qa[..., 0, :], positions), rope(qa[..., 1, :], positions)
    k1, k2 = rope(ka[..., 0, :], positions), rope(ka[..., 1, :], positions)
    lam_init = lambda_init_fn(layer)
    f32 = jnp.float32
    lam = (jnp.exp(jnp.sum(lq1.astype(f32) * lk1.astype(f32)))
           - jnp.exp(jnp.sum(lq2.astype(f32) * lk2.astype(f32))) + lam_init)
    oa = differential_attention(q1, q2, k1, k2, va.reshape(B, S, A_HEADS, A_V_DIM), lam)
    oa = rms_norm(oa, subln) * (1.0 - lam_init)
    ob = stick_breaking_attention(qs.reshape(B, S, B_HEADS, B_HEAD_DIM),
                                  ks.reshape(B, S, B_HEADS, B_HEAD_DIM),
                                  vs.reshape(B, S, B_HEADS, B_HEAD_DIM))
    o = jnp.concatenate([oa.reshape(B, S, A_WIDTH), ob.reshape(B, S, B_WIDTH)], axis=-1)
    return o @ w_out

def odd_mixer(h, positions, w_in, w_out, sinks):
    B, S, _ = h.shape
    proj = h @ w_in
    q, k, v = jnp.split(proj, [C_OUT, C_OUT + C_KV_WIDTH], axis=-1)
    q = rope(q.reshape(B, S, C_Q_HEADS, C_HEAD_DIM), positions)
    k = rope(k.reshape(B, S, C_KV_HEADS, C_HEAD_DIM), positions)
    v = v.reshape(B, S, C_KV_HEADS, C_HEAD_DIM)
    o = sliding_window_sink_attention(q, k, v, sinks)
    return o.reshape(B, S, C_OUT) @ w_out

def squared_relu_mlp(h, w_up, w_down):
    return jnp.square(jax.nn.relu(h @ w_up)) @ w_down

def setup_inputs(seed: int = 0) -> dict:
    key = jax.random.key(seed)
    ks = jax.random.split(key, 16)
    f32 = jnp.float32

    def nrm(k, shape, scale):
        return jax.random.normal(k, shape, f32) * scale

    return {
        'x': nrm(ks[0], (BATCH, SEQ, D_MODEL), 1.0),
        'positions': jnp.tile(jnp.arange(SEQ, dtype=jnp.int32)[None, :], (BATCH, 1)),
        'norm_mix': 1.0 + nrm(ks[1], (DEPTH, D_MODEL), 0.02),
        'norm_mlp': 1.0 + nrm(ks[2], (DEPTH, D_MODEL), 0.02),
        'norm_final': 1.0 + nrm(ks[3], (D_MODEL,), 0.02),
        'w_in_ab': nrm(ks[4], (N_EVEN, D_MODEL, AB_IN), D_MODEL ** -0.5),
        'w_out_ab': nrm(ks[5], (N_EVEN, AB_OUT, D_MODEL), AB_OUT ** -0.5),
        'lambda_q1': nrm(ks[6], (N_EVEN, A_HALF_DIM), 0.1),
        'lambda_k1': nrm(ks[7], (N_EVEN, A_HALF_DIM), 0.1),
        'lambda_q2': nrm(ks[8], (N_EVEN, A_HALF_DIM), 0.1),
        'lambda_k2': nrm(ks[9], (N_EVEN, A_HALF_DIM), 0.1),
        'diff_subln': 1.0 + nrm(ks[10], (N_EVEN, A_V_DIM), 0.02),
        'w_in_c': nrm(ks[11], (N_ODD, D_MODEL, C_IN), D_MODEL ** -0.5),
        'w_out_c': nrm(ks[12], (N_ODD, C_OUT, D_MODEL), C_OUT ** -0.5),
        'sinks': nrm(ks[13], (N_ODD, C_Q_HEADS), 1.0),
        'w_up': nrm(ks[14], (DEPTH, D_MODEL, D_FF), D_MODEL ** -0.5),
        'w_down': nrm(ks[15], (DEPTH, D_FF, D_MODEL), D_FF ** -0.5),
    }

def reference(x, positions, norm_mix, norm_mlp, norm_final, w_in_ab, w_out_ab,
              lambda_q1, lambda_k1, lambda_q2, lambda_k2, diff_subln,
              w_in_c, w_out_c, sinks, w_up, w_down):
    for layer in range(DEPTH):
        h = rms_norm(x, norm_mix[layer])
        j = layer // 2
        if layer % 2 == 0:
            x = x + even_mixer(h, positions, w_in_ab[j], w_out_ab[j],
                               lambda_q1[j], lambda_k1[j], lambda_q2[j], lambda_k2[j],
                               diff_subln[j], layer)
        else:
            x = x + odd_mixer(h, positions, w_in_c[j], w_out_c[j], sinks[j])
        x = x + squared_relu_mlp(rms_norm(x, norm_mlp[layer]), w_up[layer], w_down[layer])
    return rms_norm(x, norm_final)


_drawn_inputs = setup_inputs


def setup_inputs(seed=0):
    import zlib

    import numpy as np

    out = dict(_drawn_inputs(seed))
    spreads = {}
    factors = {'norm_final': 2.947,
     'lambda_q1': 4.097,
     'lambda_k2': 8.0,
     'diff_subln': 4.701,
     'sinks': 3.525}
    for name, (base, spread) in spreads.items():
        noise = np.random.default_rng([zlib.crc32(name.encode()), seed]).standard_normal(out[name].shape)
        drawn = base * np.exp(spread * noise) if base else spread * noise
        out[name] = __import__('jax').numpy.asarray(drawn.astype(out[name].dtype))
    for name, factor in factors.items():
        out[name] = (out[name] * factor).astype(out[name].dtype)
    return out
```

```python
from contextlib import ExitStack

import numpy as np

import concourse.bass as bass
from concourse import mybir

F32 = mybir.dt.float32
F32R = mybir.dt.float32r
I32 = mybir.dt.int32
ALU = mybir.AluOpType
ACT = mybir.ActivationFunctionType
AX_X = mybir.AxisListType.X

P = 128
D = 2048
S = 256
TB = S // P
KT = D // P
STEPS = 8
SK = KT // STEPS
LOADS = 4
LK = KT // LOADS
RING = 4
W = 512
WA = 384
NC = D // W
D_FF = 4 * D
SUPER = D_FF // D
HEADS_A, HEADS_B = 8, 8
HEADS = HEADS_A + HEADS_B
GROUPS, PAIRS = 4, 4
DH = 64
EPS = 1e-6
NEG = -1e30
LAM_INIT = 0.8 - 0.6
SCALE_A = DH ** -0.5
SCALE_B = 128 ** -0.5

U_AB = 0
U_OAB = U_AB + HEADS
U_MLP0 = U_OAB + NC
U_C = U_MLP0 + 2 * NC * SUPER
U_OC = U_C + 1 + GROUPS
U_MLP1 = U_OC + NC
U_END = U_MLP1 + 2 * NC * SUPER

T_X0 = 0
T_X1 = T_X0 + NC
T_H0 = T_X1 + NC
T_X2 = T_H0 + NC * SUPER
T_C = T_X2 + NC
T_X3 = T_C + GROUPS
T_H1 = T_X3 + NC


def some(start, size):
    return slice(start, start + size) if isinstance(start, int) else bass.ds(start, size)


def trunk_kernel(nc, x, positions, norm_t, norm_final, w_ab, w_oab, w_mlp, w_c, w_oc,
                 lambdas, subln, sinks, out):
    with ExitStack() as ctx:
        def sb(name, shape, dt=F32):
            return ctx.enter_context(nc.sbuf_tensor(name, shape, dt))

        def sem(name):
            return ctx.enter_context(nc.semaphore(name))

        x_sb = sb("x_sb", [P, TB, D])
        X_hi, X_lo = sb("X_hi", [P, KT, S], F32R), sb("X_lo", [P, KT, S], F32R)
        Y_hi, Y_lo = sb("Y_hi", [P, KT, S], F32R), sb("Y_lo", [P, KT, S], F32R)
        raw = sb("raw", [P, LOADS, LK * W])
        w_hi = sb("w_hi", [P, RING, SK * W], F32R)
        w_lo = sb("w_lo", [P, RING, SK * W], F32R)

        ident = sb("ident", [P, P])
        band = sb("band", [P, 3 * P])
        full = sb("full", [P, 3 * P])
        strict = sb("strict", [P, 3 * P])
        strict01 = sb("strict01", [P, P])
        neg_tri = sb("neg_tri", [P, P])
        neg_one = sb("neg_one", [P, P])
        norm_g = sb("norm_g", [P, 4, KT])
        lam_in = sb("lam_in", [P, 4, DH])
        lam = sb("lam", [P, 8])
        subln_s = sb("subln_s", [P, 2])
        sink_in = sb("sink_in", [P, 2 * GROUPS * PAIRS])
        sink8 = sb("sink8", [P, GROUPS * PAIRS, 4])
        half_pow = sb("half_pow", [P, 2])
        pos_i = sb("pos_i", [P, TB], I32)
        pos_f = sb("pos_f", [P, TB])
        inv_freq = sb("inv_freq", [P, DH // 2])
        ang = sb("ang", [P, TB, DH // 2])
        turns_i = sb("turns_i", [P, TB, DH // 2], I32)
        turns_f = sb("turns_f", [P, TB, DH // 2])
        cos = sb("cos", [P, TB, DH // 2])
        sin = sb("sin", [P, TB, DH // 2])
        nsin = sb("nsin", [P, TB, DH // 2])
        ss = sb("ss", [P, 5, TB, NC])
        ms = sb("ms", [P, 5, TB])
        rstd = sb("rstd", [P, 5, TB])
        junk = sb("junk", [P, TB, W])
        junk2 = sb("junk2", [P, TB, P])

        proj = sb("proj", [P, 2, TB * W])
        rot = sb("rot", [P, TB * W])
        rot2 = sb("rot2", [P, TB * W])
        qkT = sb("qkT", [P, 4 * S])
        kT = sb("kT", [P, S])
        sc = sb("sc", [P, 2, 2, 3 * P])
        small = sb("small", [P, 64])
        p_sb = sb("p_sb", [P, 3 * P])
        pT = sb("pT", [P, 2, 3 * P])
        o_sb = sb("o_sb", [P, TB * P])
        on_sb = sb("on_sb", [P, TB * W])
        kv = sb("kv", [P, TB, W])
        krot = sb("krot", [P, TB, GROUPS * DH])
        k_cur = sb("k_cur", [P, TB, 2, DH])
        v_cur = sb("v_cur", [P, TB, DH + 1])

        ps = [ctx.enter_context(nc.psum_tensor(f"bank{i}", [P, W], F32)) for i in range(8)]

        final_g = raw[:, 0, :]
        mx, negm, sums, rs = (small[:, 4 * i:4 * i + 4] for i in range(4))
        oss, ors = small[:, 16:18], small[:, 18:20]
        M_c = [small[:, 20 + 4 * i:24 + 4 * i] for i in range(2)]
        d_c = [small[:, 28 + 4 * i:32 + 4 * i] for i in range(2)]
        es_c = [small[:, 36 + 4 * i:40 + 4 * i] for i in range(2)]
        mx_c = [small[:, 44 + 4 * i:48 + 4 * i] for i in range(2)]
        den, rden = small[:, 52:56], small[:, 56:60]
        sp_a, sp, wm, wT = sc[:, 0, 0, :], sc[:, 0, 1, :], sc[:, 1, 0, :], sc[:, 1, 1, :]

        def qkv(par):
            return proj[:, par, 0:TB * WA].rearrange("p (t c) -> p t c", t=TB)

        def wide(par):
            return proj[:, par, :].rearrange("p (t c) -> p t c", t=TB)

        consts = sem("consts")
        x_landed = [sem(f"x_landed{c}") for c in range(NC)]
        made_part, made = sem("made_part"), sem("made")
        trig_v, trig_a, trig = sem("trig_v"), sem("trig_a"), sem("trig")
        w_landed = [sem(f"w_landed{j}") for j in range(LOADS)]
        hi_ready, lo_ready = sem("hi_ready"), sem("lo_ready")
        steps_done = sem("steps_done")
        proj_ready = sem("proj_ready")
        x_added = sem("x_added")
        relu_ready = sem("relu_ready")
        hid_ready = sem("hid_ready")
        turned = sem("turned")
        turn_hi, turn_lo = sem("turn_hi"), sem("turn_lo")
        squared = sem("squared")
        stat_v, stat_ready = sem("stat_v"), sem("stat_ready")
        rope_part, rope_ready = sem("rope_part"), sem("rope_ready")
        qkT_done, qkT_ready = sem("qkT_done"), sem("qkT_ready")
        scores_done = sem("scores_done")
        max_part, max_ready, negm_ready = sem("max_part"), sem("max_ready"), sem("negm_ready")
        exp_done = sem("exp_done")
        p_part, p_ready = sem("p_part"), sem("p_ready")
        pT_done, pT_ready = sem("pT_done"), sem("pT_ready")
        pv_done, o_ready = sem("pv_done"), sem("o_ready")
        oss_ready, ors_ready, on_ready = sem("oss_ready"), sem("ors_ready"), sem("on_ready")
        oT_done, y_hi, y_lo = sem("oT_done"), sem("y_hi"), sem("y_lo")
        soft_part, soft_done = sem("soft_part"), sem("soft_done")
        sp_part, sp_ready = sem("sp_part"), sem("sp_ready")
        w_done, wm_ready, wexp_done = sem("w_done"), sem("wm_ready"), sem("wexp_done")
        c_scores, c_max, c_m, c_d = sem("c_scores"), sem("c_max"), sem("c_m"), sem("c_d")
        c_sub, c_exp = sem("c_sub"), sem("c_exp")
        c_pT, c_pT_a, c_pT_v = sem("c_pT"), sem("c_pT_a"), sem("c_pT_v")
        c_pv, c_den, c_on = sem("c_pv"), sem("c_den"), sem("c_on")
        fin, stored = sem("fin"), sem("stored")

        block = ctx.enter_context(nc.Block())

        @block.sync
        def _(sp_):
            def load(src, first, U, wd, wait):
                for j in range(LOADS):
                    if wait:
                        sp_.wait_ge(lo_ready, 8 * U - 6 + 2 * j)
                    sp_.dma_start(raw[:, j, 0:LK * wd], src[first + j]).then_inc(w_landed[j], 16)

            for c in range(NC):
                sp_.dma_start(x_sb[:, :, c * W:(c + 1) * W],
                              x.rearrange("(t p) d -> p t d", p=P)[:, :, c * W:(c + 1) * W]).then_inc(x_landed[c], 16)
                if c == 0:
                    sp_.dma_start(norm_g[:, :, :], norm_t).then_inc(consts, 16)
                sp_.dma_start(raw[:, c, 0:LK * WA], w_ab[c]).then_inc(w_landed[c], 16)
            sp_.dma_start(pos_i[:, :], positions).then_inc(consts, 16)
            sp_.dma_start(lam_in[:, :, :].rearrange("p a b -> p (a b)"), lambdas).then_inc(consts, 16)
            sp_.dma_start(subln_s[:, 0:1], subln).then_inc(consts, 16)
            sp_.dma_start(sink_in[:, :], sinks).then_inc(consts, 16)
            with sp_.Fori(1, HEADS) as i:
                load(w_ab, 4 * i, i, WA, True)
            with sp_.Fori(0, NC) as i:
                load(w_oab, 4 * i, U_OAB + i, W, True)
            with sp_.Fori(0, 2 * NC * SUPER) as i:
                load(w_mlp, 4 * i, U_MLP0 + i, W, True)
            with sp_.Fori(0, 1 + GROUPS) as i:
                load(w_c, 4 * i, U_C + i, W, True)
            with sp_.Fori(0, NC) as i:
                load(w_oc, 4 * i, U_OC + i, W, True)
            with sp_.Fori(0, 2 * NC * SUPER) as i:
                load(w_mlp, 4 * (2 * NC * SUPER) + 4 * i, U_MLP1 + i, W, True)
            sp_.wait_ge(lo_ready, 8 * U_END - 6)
            sp_.dma_start(final_g, norm_final).then_inc(w_landed[0], 16)
            for c in range(TB):
                sp_.wait_ge(fin, c + 1)
                sp_.dma_start(out.rearrange("(t p) d -> p t d", p=P)[:, c, :], x_sb[:, c, :]).then_inc(stored, 16)
            sp_.wait_ge(stored, 16 * TB)

        @block.tensor
        def _(pe):
            def step(U, k, par, A, wd, inputs=None, free=None):
                pe.wait_ge(lo_ready, 8 * U + k + 1)
                if inputs is not None:
                    pe.wait_ge(inputs[0], inputs[1])
                if k == 0 and free is not None:
                    pe.wait_ge(free[0], free[1])
                A_hi, A_lo = A
                slot = k % RING
                for t in range(TB):
                    for q in range(SK):
                        kt = SK * k + q
                        rh = w_hi[:, slot, q * wd:(q + 1) * wd]
                        rl = w_lo[:, slot, q * wd:(q + 1) * wd]
                        o = ps[2 * par + t][:, 0:wd]
                        cols = slice(t * P, (t + 1) * P)
                        pe.matmul(o, A_lo[:, kt, cols], rh, start=(kt == 0), stop=False)
                        pe.matmul(o, A_hi[:, kt, cols], rl, start=False, stop=False)
                        last = pe.matmul(o, A_hi[:, kt, cols], rh, start=False, stop=(kt == KT - 1))
                last.then_inc(steps_done, 1)

            def turn(n, ready, value, src):
                pe.wait_ge(ready, value)
                if not isinstance(n, int) or n > 0:
                    pe.wait_ge(turn_lo, 2 * n)
                for b in range(2):
                    for q in range(2):
                        for t in range(TB):
                            kt = 2 * b + q
                            last = pe.transpose(ps[4 + b][:, q * S + t * P:q * S + (t + 1) * P],
                                                src[:, t, kt * P:(kt + 1) * P], ident[:, :])
                    last.then_inc(turned, 1)

            def diff_turn(h, first=False):
                pe.wait_ge(rope_ready, h + 1)
                if not first:
                    pe.wait_ge(y_lo, h - 1)
                for b, (t, c) in enumerate(((0, 0), (1, 0), (0, 1), (1, 1))):
                    last = pe.transpose(ps[4][:, b * P:(b + 1) * P],
                                        rot[:, t * S + c * P:t * S + (c + 1) * P], ident[:, :])
                last.then_inc(qkT_done, 1)

            def diff_scores(h, first=False):
                pe.wait_ge(qkT_ready, h + 1)
                if not first:
                    pe.wait_ge(max_ready, h)
                for q0, keys, at in ((0, P, 0), (P, S, P)):
                    for m in range(2):
                        r = slice(DH * m, DH * (m + 1))
                        last = pe.matmul(ps[5 + m][:, at:at + keys], qkT[r, q0:q0 + P], qkT[r, S:S + keys],
                                         start=True, stop=True)
                last.then_inc(scores_done, 1)

            def diff_pT(h, first=False):
                pe.wait_ge(p_ready, h + 1)
                if not first:
                    pe.wait_ge(o_ready, h)
                for b in range(3):
                    last = pe.transpose(ps[7][:, b * P:(b + 1) * P], p_sb[:, b * P:(b + 1) * P], ident[:, :])
                last.then_inc(pT_done, 1)

            def diff_pv(h, par):
                pe.wait_ge(pT_ready, h + 1)
                v = qkv(par)
                pe.matmul(ps[7][:, 0:P], pT[:, 0, 0:P], v[:, 0, S:WA], start=True, stop=True)
                pe.matmul(ps[7][:, P:S], pT[:, 0, P:S], v[:, 0, S:WA], start=True, stop=False)
                pe.matmul(ps[7][:, P:S], pT[:, 0, S:3 * P], v[:, 1, S:WA], start=False, stop=True).then_inc(pv_done, 1)

            def diff_oT(h):
                pe.wait_ge(on_ready, h + 1)
                pe.wait_ge(qkT_ready, h + 2)
                for t in range(TB):
                    last = pe.transpose(ps[4][:, t * P:(t + 1) * P], on_sb[:, t * P:(t + 1) * P], ident[:, :])
                last.then_inc(oT_done, 1)

            def stick_turn(h, par):
                pe.wait_ge(proj_ready, h + 1)
                pe.wait_ge(y_lo, h - 1)
                pe.wait_ge(qkT_ready, h)
                v = qkv(par)
                for b, (t, c) in enumerate(((0, 0), (1, 0), (0, 1), (1, 1))):
                    last = pe.transpose(ps[4][:, b * P:(b + 1) * P], v[:, t, c * P:(c + 1) * P], ident[:, :])
                last.then_inc(qkT_done, 1)

            def stick_z(h, first=False):
                pe.wait_ge(qkT_ready, h + 1)
                if first:
                    pe.wait_ge(max_ready, HEADS_A)
                else:
                    pe.wait_ge(sp_ready, h - HEADS_A)
                pe.matmul(ps[5][:, 0:S], qkT[:, S:S + P], qkT[:, 0:S], start=True, stop=True)
                pe.matmul(ps[5][:, S:3 * P], qkT[:, S + P:2 * S], qkT[:, P:S],
                          start=True, stop=True).then_inc(scores_done, 1)

            def stick_sum(h, first=False):
                pe.wait_ge(sp_ready, h - HEADS_A + 1)
                if not first:
                    pe.wait_ge(wm_ready, h - HEADS_A)
                pe.matmul(ps[6][:, 0:S], qkT[:, S:S + P], qkT[:, 0:S], start=True, stop=False)
                pe.matmul(ps[6][:, 0:S], neg_tri[:, :], sp[:, 0:S], start=False, stop=False)
                pe.matmul(ps[6][:, P:S], neg_one[:, :], sp[:, S:3 * P], start=False, stop=True)
                pe.matmul(ps[6][:, S:3 * P], qkT[:, S + P:2 * S], qkT[:, P:S], start=True, stop=False)
                pe.matmul(ps[6][:, S:3 * P], neg_tri[:, :], sp[:, S:3 * P],
                          start=False, stop=True).then_inc(w_done, 1)

            def stick_pv(h, par, first=False):
                pe.wait_ge(wexp_done, h - HEADS_A + 1)
                if first:
                    pe.wait_ge(o_ready, HEADS_A)
                else:
                    pe.wait_ge(y_lo, h)
                v = qkv(par)
                pe.matmul(ps[7][:, 0:S], v[:, 0, S:WA], wT[:, 0:S], start=True, stop=False)
                pe.matmul(ps[7][:, P:S], v[:, 1, S:WA], wT[:, S:3 * P], start=False, stop=True).then_inc(pv_done, 1)

            def win_turn(g):
                pe.wait_ge(rope_ready, HEADS_A + 2 + g)
                pe.wait_ge(turn_lo, 2 * (T_C + g))
                for hp in range(PAIRS):
                    for t in range(TB):
                        pe.transpose(ps[4 + hp // 2][:, (hp % 2) * S + t * P:(hp % 2) * S + (t + 1) * P],
                                     rot[:, t * W + hp * P:t * W + (hp + 1) * P], ident[:, :])
                for t in range(TB):
                    last = pe.transpose(ps[6][:, t * P:(t + 1) * P],
                                        k_cur[:, t].rearrange("p a b -> p (a b)"), ident[:, :])
                last.then_inc(qkT_done, 1)

            def win_scores(g, j):
                pe.wait_ge(qkT_ready, HEADS + 1 + g)
                if not (isinstance(g, int) and g == 0 and j == 0):
                    pe.wait_ge(c_max, PAIRS * g + j)
                for q0, keys, at in ((0, P, 0), (P, S, P)):
                    for e in range(2):
                        r = slice(DH * e, DH * (e + 1))
                        last = pe.matmul(ps[6 + e][:, at:at + keys], qkT[r, j * S + q0:j * S + q0 + P],
                                         kT[r, 0:keys], start=True, stop=True)
                last.then_inc(c_scores, 1)

            def win_pT(g, j):
                pe.wait_ge(c_exp, PAIRS * g + j + 1)
                if not (isinstance(g, int) and g == 0 and j == 0):
                    pe.wait_ge(c_pT_a, PAIRS * g + j)
                    pe.wait_ge(c_pT_v, PAIRS * g + j)
                for e in range(2):
                    for b in range(3):
                        last = pe.transpose(ps[4 + e][:, b * P:(b + 1) * P],
                                            sc[:, j % 2, e, b * P:(b + 1) * P], ident[:, :])
                last.then_inc(c_pT, 1)

            def win_pv(g, j):
                n = PAIRS * g + j
                pe.wait_ge(c_pT_a, n + 1)
                pe.wait_ge(c_pT_v, n + 1)
                if not (isinstance(n, int) and n == 0):
                    pe.wait_ge(c_on, n)
                C = DH + 1
                for e in range(2):
                    o0, o1 = (ps[2][:, (2 * e + q) * C:(2 * e + q + 1) * C] for q in range(2))
                    pe.matmul(o0, pT[:, e, 0:P], v_cur[:, 0, :], start=True, stop=True)
                    pe.matmul(o1, pT[:, e, P:2 * P], v_cur[:, 0, :], start=True, stop=False)
                    last = pe.matmul(o1, pT[:, e, 2 * P:3 * P], v_cur[:, 1, :], start=False, stop=True)
                last.then_inc(c_pv, 1)

            def win_hooks(k, g, old, last=False):
                if old is not None and k == 0:
                    win_pv(old, 3)
                if old is not None and k == 1:
                    turn(T_C + old, c_on, PAIRS * old + PAIRS, on_c)
                if g is None:
                    return
                if k == 2:
                    win_turn(g)
                if k >= 3 and not (last and k > 5):
                    if k <= 6:
                        win_scores(g, k - 3)
                    if k >= 4:
                        win_pT(g, k - 4)
                    if k >= 5:
                        win_pv(g, k - 5)
                if last and k == 5:
                    win_scores(g, 3)
                    win_pT(g, 2)
                    win_pv(g, 1)
                    win_pT(g, 3)
                    win_pv(g, 2)
                    win_pv(g, 3)
                    turn(T_C + g, c_on, PAIRS * g + PAIRS, on_c)

            on_c = on_sb[:, :].rearrange("p (t c) -> p t c", t=TB)
            Xs, Ys = (X_hi, X_lo), (Y_hi, Y_lo)

            pe.wait_ge(made, 1)
            for c in range(NC):
                turn(T_X0 + c, x_landed[c], 16, x_sb[:, :, c * W:(c + 1) * W])

            def unit_ab(U, par, diff=None, old=None, stick=None, first=False, first_stick=False):
                for k in range(STEPS):
                    inputs = (turn_lo, 2 * T_X0 + k + 1) if first else None
                    free = None if isinstance(U, int) and U < 2 else (proj_ready, U - 1)
                    step(U, k, par, Xs, WA, inputs, free)
                    hooks_ab(k, par, diff, old, stick, first_stick)

            def hooks_ab(k, par, diff, old, stick, first_stick):
                if old is not None and k == 1:
                    diff_pT(old, first=isinstance(old, int) and old == 0)
                if stick is not None and k == 1:
                    stick_turn(stick, 1 - par)
                if old is not None and k == 2:
                    diff_pv(old, par)
                if stick is not None and k == 2:
                    stick_z(stick, first_stick)
                if diff is not None and k == 3:
                    diff_turn(diff, first=isinstance(diff, int) and diff < 2)
                if diff is not None and k == 4:
                    diff_scores(diff, first=isinstance(diff, int) and diff == 0)
                if stick is not None and k == 4:
                    stick_sum(stick, first_stick)
                if old is not None and k == 6:
                    diff_oT(old)
                if stick is not None and k == 6:
                    stick_pv(stick, 1 - par, first_stick)

            unit_ab(0, 0, first=True)
            unit_ab(1, 1, diff=0)
            unit_ab(2, 0, diff=1, old=0)
            unit_ab(3, 1, diff=2, old=1)
            with pe.Fori(2, HEADS_A // 2) as i:
                unit_ab(2 * i, 0, diff=2 * i - 1, old=2 * i - 2)
                unit_ab(2 * i + 1, 1, diff=2 * i, old=2 * i - 1)
            unit_ab(8, 0, diff=7, old=6)
            unit_ab(9, 1, old=7, stick=8, first_stick=True)
            with pe.Fori(5, HEADS // 2) as i:
                unit_ab(2 * i, 0, stick=2 * i - 1)
                unit_ab(2 * i + 1, 1, stick=2 * i)

            for n in range(NC):
                U, par = U_OAB + n, n % 2
                for k in range(STEPS):
                    step(U, k, par, Ys, W, (y_lo, 2 * k + 2) if n == 0 else None,
                         (proj_ready, U - 1) if n < 2 else (x_added, n - 1))
                    if n == 0:
                        hooks_ab(k, par, None, None, HEADS - 1, False)
                    elif k == 2:
                        turn(T_X1 + n - 1, x_added, n, x_sb[:, :, (n - 1) * W:n * W])

            def mlp(s, U0, T_in, T_h, adds, relus, first, last):
                a, r = adds + NC * s, relus + NC * s
                for n in range(2 * NC):
                    U, par = U0 + 2 * NC * s + n, n % 2
                    up = n < NC
                    for k in range(STEPS):
                        inputs = None
                        if n == 0 and first:
                            inputs = (turn_lo, 2 * T_in + k + 1)
                        if n == NC:
                            inputs = (turn_lo, 2 * (T_h + NC * s) + k + 1)
                        if n in (0, 1):
                            free = (x_added, a - 1 + n)
                        elif n < NC + 2:
                            free = (relu_ready, r + n - 1)
                        else:
                            free = (x_added, a + n - NC - 1)
                        step(U, k, par, Xs if up else Ys, W, inputs, free)
                        if n == 0 and first and k == 2:
                            turn(T_in + NC - 1, x_added, a, x_sb[:, :, (NC - 1) * W:NC * W])
                        if 1 <= n <= NC and k == 3:
                            turn(T_h + NC * s + n - 1, hid_ready, r + n, wide((n - 1) % 2))
                        if n > NC and last and k == 2:
                            turn(T_h + NC * SUPER + n - NC - 1, x_added, a + n - NC,
                                 x_sb[:, :, (n - NC - 1) * W:(n - NC) * W])

            def mlps(U0, T_in, T_h, adds, relus, turns_after):
                mlp(0, U0, T_in, T_h, adds, relus, True, False)
                with pe.Fori(1, SUPER - 1) as s:
                    mlp(s, U0, T_in, T_h, adds, relus, False, False)
                mlp(SUPER - 1, U0, T_in, T_h, adds, relus, False, turns_after)

            mlps(U_MLP0, T_X1, T_H0, NC, 0, True)

            def unit_c(U, hooks, free, first=False):
                for k in range(STEPS):
                    step(U, k, 0, Xs, W, (turn_lo, 2 * T_X2 + k + 1) if first else None, free)
                    if first and k == 2:
                        turn(T_X2 + NC - 1, x_added, NC + NC * SUPER, x_sb[:, :, (NC - 1) * W:NC * W])
                    if hooks is not None:
                        win_hooks(k, *hooks)

            unit_c(U_C, None, (x_added, NC + NC * SUPER - 1), first=True)
            unit_c(U_C + 1, None, (proj_ready, HEADS + 1))
            unit_c(U_C + 2, (0, None), (proj_ready, HEADS + 2))
            with pe.Fori(1, GROUPS - 1) as g:
                unit_c(U_C + 2 + g, (g, g - 1), (proj_ready, HEADS + 2 + g))

            added = NC + NC * SUPER
            for n in range(NC):
                U, par = U_OC + n, n % 2
                for k in range(STEPS):
                    free = ((proj_ready, HEADS + 1 + GROUPS), (c_on, GROUPS * PAIRS),
                            (x_added, added + 1), (x_added, added + 2))[n]
                    step(U, k, par, Ys, W, (turn_lo, 2 * T_C + k + 1) if n == 0 else None, free)
                    if n == 0:
                        win_hooks(k, GROUPS - 1, GROUPS - 2, last=True)
                    elif k == 2:
                        turn(T_X3 + n - 1, x_added, added + n, x_sb[:, :, (n - 1) * W:n * W])

            mlps(U_MLP1, T_X3, T_H1, added + NC, NC * SUPER, False)

        @block.scalar
        def _(act):
            def split(U, k, wd):
                if k >= STEPS:
                    U, k = U + 1, k - STEPS
                if k % 2 == 0:
                    act.wait_ge(w_landed[k // 2], 16 * U + 16)
                if not isinstance(U, int) or 8 * U + k >= RING:
                    act.wait_ge(steps_done, 8 * U + k - RING + 1)
                act.activation(w_hi[:, k % RING, 0:SK * wd],
                               raw[:, k // 2, (k % 2) * SK * wd:(k % 2 + 1) * SK * wd],
                               ACT.Copy).then_inc(hi_ready, 1)

            def turn_high(n, kt0, A_hi, g=None):
                for b in range(2):
                    act.wait_ge(turned, 2 * n + b + 1)
                    if g is None:
                        last = act.activation(A_hi[:, some(kt0 + 2 * b, 2), :],
                                              ps[4 + b][:, :].rearrange("p (a b) -> p a b", a=2), ACT.Copy)
                    else:
                        for q in range(2):
                            kt = kt0 + 2 * b + q
                            last = act.activation(A_hi[:, kt, :], ps[4 + b][:, q * S:(q + 1) * S], ACT.Copy,
                                                  scale=norm_g[:, g, kt:kt + 1])
                    last.then_inc(turn_hi, 1)

            def squares(i, c, ready, value):
                act.wait_ge(ready, value)
                if i or c:
                    act.wait_ge(squared, NC * i + c)
                for t in range(TB):
                    last = act.activation(junk[:, t, :], x_sb[:, t, c * W:(c + 1) * W], ACT.Square,
                                          accum_out=ss[:, i, t, c:c + 1])
                last.then_inc(squared, 1)

            def evacuate(U, par, dst, wd, func, i, done):
                act.wait_ge(steps_done, 8 * U + 8)
                for t in range(TB):
                    last = act.activation(dst[:, t, 0:wd], ps[2 * par + t][:, 0:wd], func,
                                          scale=rstd[:, i, t:t + 1])
                last.then_inc(done, 1)

            act.wait_ge(consts, 80)
            act.wait_ge(trig_v, 9)
            act.activation(cos[:, :, :], ang[:, :, :], ACT.Sin, scale=0.5)
            act.activation(sin[:, :, :], ang[:, :, :], ACT.Sin)
            act.activation(nsin[:, :, :], ang[:, :, :], ACT.Sin, scale=-1.0).then_inc(trig_a, 1)
            act.wait_ge(trig_v, 12)
            act.activation(lam[:, 2:4], lam[:, 0:2], ACT.Exp).then_inc(trig_a, 1)
            for c in range(NC):
                turn_high(T_X0 + c, 4 * c, X_hi, 0)
                squares(0, c, x_landed[c], 16)
            split(0, 0, WA)
            split(0, 1, WA)
            split(0, 2, WA)
            split(0, 3, WA)

            def slot_ab(k, diff=None, old=None, stick=None, first_stick=False):
                if old is not None and k == 1:
                    act.wait_ge(pT_done, old + 1)
                    act.activation(pT[:, 0, :], ps[7][:, 0:3 * P], ACT.Copy).then_inc(pT_ready, 1)
                if old is not None and k == 3:
                    act.wait_ge(pv_done, old + 1)
                    if not isinstance(old, int) or old > 0:
                        act.wait_ge(on_ready, old)
                    act.activation(o_sb[:, :], ps[7][:, 0:S], ACT.Copy).then_inc(o_ready, 1)
                if diff is not None and k == 4:
                    act.wait_ge(qkT_done, diff + 1)
                    if not isinstance(diff, int) or diff > 0:
                        act.wait_ge(scores_done, diff)
                    act.activation(qkT[:, 0:2 * S], ps[4][:, :], ACT.Copy).then_inc(qkT_ready, 1)
                if diff is not None and k == 6:
                    act.wait_ge(negm_ready, diff + 1)
                    for m in range(2):
                        for q, r in ((0, slice(0, P)), (1, slice(P, 3 * P))):
                            c = 2 * m + q
                            last = act.activation(sc[:, 0, m, r], sc[:, 0, m, r], ACT.Exp, bias=negm[:, c:c + 1],
                                                  scale=SCALE_A, accum_out=sums[:, c:c + 1])
                    last.then_inc(exp_done, 1)
                if stick is not None and k == 2:
                    act.wait_ge(qkT_done, stick + 1)
                    if first_stick:
                        act.wait_ge(scores_done, HEADS_A)
                    else:
                        act.wait_ge(w_done, stick - HEADS_A)
                    act.activation(qkT[:, 0:S], ps[4][:, 0:S], ACT.Copy, scale=SCALE_B)
                    act.activation(qkT[:, S:2 * S], ps[4][:, S:2 * S], ACT.Copy).then_inc(qkT_ready, 1)
                if stick is not None and k == 3:
                    j = stick - HEADS_A
                    act.wait_ge(scores_done, stick + 1)
                    if first_stick:
                        act.wait_ge(p_ready, HEADS_A)
                    else:
                        act.wait_ge(sp_ready, j)
                    act.activation(sp_a, ps[5][:, 0:3 * P], ACT.Abs).then_inc(soft_part, 1)
                    act.wait_ge(soft_part, 2 * j + 1)
                    act.activation(sp_a, sp_a, ACT.Exp, scale=-1.0).then_inc(soft_part, 1)
                    act.wait_ge(soft_part, 2 * j + 2)
                    act.activation(sp_a, sp_a, ACT.Ln, bias=1.0).then_inc(soft_done, 1)
                if stick is not None and k == 5:
                    act.wait_ge(wm_ready, stick - HEADS_A + 1)
                    act.wait_ge(pv_done, stick)
                    act.activation(wT, wm, ACT.Exp).then_inc(wexp_done, 1)
                if old is not None and k == 6:
                    act.wait_ge(oT_done, old + 1)
                    act.activation(Y_hi[:, old, :], ps[4][:, 0:S], ACT.Copy, scale=subln_s[:, 1:2]).then_inc(y_hi, 1)
                if stick is not None and k == 6:
                    act.wait_ge(pv_done, stick + 1)
                    act.activation(Y_hi[:, stick, :], ps[7][:, 0:S], ACT.Copy).then_inc(y_hi, 1)

            def unit_ab(U, par, wd_next=WA, **heads):
                for k in range(STEPS):
                    split(U, k + RING, WA if k + RING < STEPS else wd_next)
                    slot_ab(k, **heads)
                if isinstance(U, int) and U == 0:
                    act.wait_ge(stat_ready, 1)
                if not isinstance(U, int) or U >= 2:
                    act.wait_ge(pv_done, U - 1)
                evacuate(U, par, qkv(par), WA, ACT.Copy, 0, proj_ready)

            unit_ab(0, 0)
            unit_ab(1, 1, diff=0)
            unit_ab(2, 0, diff=1, old=0)
            unit_ab(3, 1, diff=2, old=1)
            with act.Fori(2, HEADS_A // 2) as i:
                unit_ab(2 * i, 0, diff=2 * i - 1, old=2 * i - 2)
                unit_ab(2 * i + 1, 1, diff=2 * i, old=2 * i - 1)
            unit_ab(8, 0, diff=7, old=6)
            unit_ab(9, 1, old=7, stick=8, first_stick=True)
            with act.Fori(5, HEADS // 2 - 1) as i:
                unit_ab(2 * i, 0, stick=2 * i - 1)
                unit_ab(2 * i + 1, 1, stick=2 * i)
            unit_ab(14, 0, stick=13)
            unit_ab(15, 1, wd_next=W, stick=14)

            for n in range(NC):
                U = U_OAB + n
                for k in range(STEPS):
                    split(U, k + RING, W)
                    if n == 0:
                        slot_ab(k, stick=HEADS - 1)
                    if n > 0 and k == 1:
                        squares(1, n - 1, x_added, n)
                    if n > 0 and k == 3:
                        turn_high(T_X1 + n - 1, 4 * (n - 1), X_hi, 1)

            def mlp(s, U0, T_in, T_h, adds, relus, norm, first, last, very_last):
                a, r = adds + NC * s, relus + NC * s
                for n in range(2 * NC):
                    U, par = U0 + 2 * NC * s + n, n % 2
                    for k in range(STEPS):
                        if not (very_last and n == 2 * NC - 1 and k + RING >= STEPS):
                            split(U, k + RING, W)
                        if n == 0 and first and k == 1:
                            squares(norm, NC - 1, x_added, a)
                        if n == 0 and first and k == 3:
                            turn_high(T_in + NC - 1, 4 * (NC - 1), X_hi, norm)
                        if 1 <= n <= NC and k == 4:
                            turn_high(T_h + NC * s + n - 1, 4 * (n - 1), Y_hi)
                        if n > NC and (last or very_last) and k == 1:
                            squares(norm + 1, n - NC - 1, x_added, a + n - NC)
                        if n > NC and last and k == 3:
                            turn_high(T_h + NC * SUPER + n - NC - 1, 4 * (n - NC - 1), X_hi, norm + 1)
                    if n < NC:
                        if n == 0 and first:
                            act.wait_ge(stat_ready, norm + 1)
                        act.wait_ge(turned, 2 * (T_h + NC * s + n - 1))
                        evacuate(U, par, wide(n % 2), W, ACT.Relu, norm, relu_ready)

            def mlps(U0, T_in, T_h, adds, relus, norm, final):
                mlp(0, U0, T_in, T_h, adds, relus, norm, True, False, False)
                with act.Fori(1, SUPER - 1) as s:
                    mlp(s, U0, T_in, T_h, adds, relus, norm, False, False, False)
                mlp(SUPER - 1, U0, T_in, T_h, adds, relus, norm, False, not final, final)

            mlps(U_MLP0, T_X1, T_H0, NC, 0, 1, False)

            def win_slot(k, g, old, last=False):
                def evac_pT(g, j):
                    n = PAIRS * g + j
                    act.wait_ge(c_pT, n + 1)
                    if not (isinstance(n, int) and n == 0):
                        act.wait_ge(c_pv, n)
                    act.activation(pT[:, 0, :], ps[4][:, 0:3 * P], ACT.Copy).then_inc(c_pT_a, 1)

                def exps(g, j):
                    act.wait_ge(c_sub, PAIRS * g + j + 1)
                    act.activation(sc[:, j % 2].rearrange("p a b -> p (a b)"),
                                   sc[:, j % 2].rearrange("p a b -> p (a b)"), ACT.Exp, scale=SCALE_A)
                    act.wait_ge(c_d, PAIRS * g + j + 1)
                    if not isinstance(g, int) or PAIRS * g + j >= 2:
                        act.wait_ge(c_den, 2 * (PAIRS * g + j) - 3)
                    act.activation(es_c[j % 2], d_c[j % 2], ACT.Exp, scale=SCALE_A).then_inc(c_exp, 1)

                if old is not None and k == 1:
                    turn_high(T_C + old, 4 * old, Y_hi)
                if g is None:
                    return
                if k == 2:
                    act.wait_ge(qkT_done, HEADS + 1 + g)
                    act.activation(kT[:, :], ps[6][:, 0:S], ACT.Copy)
                    for b in range(2):
                        last_ = act.activation(qkT[:, b * 2 * S:(b + 1) * 2 * S], ps[4 + b][:, :], ACT.Copy)
                    last_.then_inc(qkT_ready, 1)
                if k >= 3 and not (last and k > 5):
                    if k >= 4:
                        evac_pT(g, k - 4)
                    if k <= 6:
                        exps(g, k - 3)
                if last and k == 5:
                    evac_pT(g, 2)
                    exps(g, 3)
                    evac_pT(g, 3)
                    turn_high(T_C + g, 4 * g, Y_hi)

            def unit_c(U, dst, hooks, first=False):
                for k in range(STEPS):
                    split(U, k + RING, W)
                    if first and k == 1:
                        squares(2, NC - 1, x_added, NC + NC * SUPER)
                    if first and k == 3:
                        turn_high(T_X2 + NC - 1, 4 * (NC - 1), X_hi, 2)
                    if hooks is not None:
                        win_slot(k, *hooks)
                if first:
                    act.wait_ge(stat_ready, 3)
                else:
                    act.wait_ge(rope_ready, U - U_C + HEADS_A)
                evacuate(U, 0, dst, W, ACT.Copy, 2, proj_ready)

            unit_c(U_C, kv[:, :, :], None, first=True)
            unit_c(U_C + 1, wide(0), None)
            unit_c(U_C + 2, wide(0), (0, None))
            with act.Fori(1, GROUPS - 1) as g:
                unit_c(U_C + 2 + g, wide(0), (g, g - 1))

            for n in range(NC):
                U = U_OC + n
                for k in range(STEPS):
                    split(U, k + RING, W)
                    if n == 0:
                        win_slot(k, GROUPS - 1, GROUPS - 2, last=True)
                    if n > 0 and k == 1:
                        squares(3, n - 1, x_added, NC + NC * SUPER + n)
                    if n > 0 and k == 3:
                        turn_high(T_X3 + n - 1, 4 * (n - 1), X_hi, 3)

            mlps(U_MLP1, T_X3, T_H1, 2 * NC + NC * SUPER, NC * SUPER, 3, True)
            squares(4, NC - 1, x_added, 2 * NC + 2 * NC * SUPER)

        @block.vector
        def _(dve):
            def split(U, k, wd):
                if k >= STEPS:
                    U, k = U + 1, k - STEPS
                dve.wait_ge(hi_ready, 8 * U + k + 1)
                dve.tensor_tensor(w_lo[:, k % RING, 0:SK * wd],
                                  raw[:, k // 2, (k % 2) * SK * wd:(k % 2 + 1) * SK * wd],
                                  w_hi[:, k % RING, 0:SK * wd].bitcast(F32), ALU.subtract).then_inc(lo_ready, 1)

            def turn_low(n, kt0, A, g=None):
                A_hi, A_lo = A
                for b in range(2):
                    dve.wait_ge(turn_hi, 2 * n + b + 1)
                    if g is None:
                        at = some(kt0 + 2 * b, 2)
                        last = dve.tensor_tensor(A_lo[:, at, :], ps[4 + b][:, :].rearrange("p (a b) -> p a b", a=2),
                                                 A_hi[:, at, :].bitcast(F32), ALU.subtract)
                    else:
                        for q in range(2):
                            kt = kt0 + 2 * b + q
                            last = dve.scalar_tensor_tensor(out=A_lo[:, kt, :], in0=ps[4 + b][:, q * S:(q + 1) * S],
                                                            scalar=norm_g[:, g, kt:kt + 1],
                                                            in1=A_hi[:, kt, :].bitcast(F32),
                                                            op0=ALU.mult, op1=ALU.subtract)
                    last.then_inc(turn_lo, 1)

            def add(U, par, n, before):
                dve.wait_ge(steps_done, 8 * U + 8)
                if not isinstance(before, int) or before >= NC:
                    dve.wait_ge(x_added, before - NC + 1)
                for t in range(TB):
                    xc = x_sb[:, t, n * W:(n + 1) * W]
                    last = dve.tensor_tensor(xc, ps[2 * par + t][:, :], xc, ALU.add)
                last.then_inc(x_added, 1)

            def stat(i):
                dve.wait_ge(squared, NC * (i + 1))
                dve.tensor_reduce(ms[:, i, :], ss[:, i, :, :], AX_X, ALU.add).then_inc(stat_v, 1)
                dve.wait_ge(stat_v, 2 * i + 1)
                dve.tensor_scalar(ms[:, i, :], ms[:, i, :], 1.0 / D, EPS, ALU.mult, ALU.add).then_inc(stat_v, 1)

            dve.wait_ge(made, 1)
            dve.wait_ge(consts, 80)
            dve.tensor_copy(pos_f[:, :], pos_i[:, :]).then_inc(trig_v, 1)
            dve.wait_ge(trig_v, 1)
            for t in range(TB):
                dve.tensor_scalar(ang[:, t, :], inv_freq[:, :], pos_f[:, t:t + 1], None, ALU.mult).then_inc(trig_v, 1)
            dve.wait_ge(trig_v, 3)
            flat = "p t c -> p (t c)"
            a2, i2, f2 = (v[:, :, :].rearrange(flat) for v in (ang, turns_i, turns_f))
            dve.tensor_scalar(i2, a2, 1.0 / (2.0 * np.pi), None, ALU.mult).then_inc(trig_v, 1)
            dve.wait_ge(trig_v, 4)
            dve.tensor_copy(f2, i2).then_inc(trig_v, 1)
            parts = [6.28125]
            parts.append(float(np.float32(np.round((2 * np.pi - parts[0]) * 2 ** 21) / 2 ** 21)))
            parts.append(float(np.float32(2 * np.pi - parts[0] - parts[1])))
            for j, part in enumerate(parts):
                dve.wait_ge(trig_v, 5 + j)
                dve.scalar_tensor_tensor(out=a2, in0=f2, scalar=-part, in1=a2,
                                         op0=ALU.mult, op1=ALU.add).then_inc(trig_v, 1)
            dve.wait_ge(trig_v, 8)
            lim = 3.1415925
            dve.tensor_scalar(a2, a2, -lim, lim, ALU.max, ALU.min).then_inc(trig_v, 1)
            for j in range(2):
                dve.tensor_tensor_reduce(out=junk2[:, j, 0:DH], in0=lam_in[:, 2 * j, :], in1=lam_in[:, 2 * j + 1, :],
                                         scale=1.0, scalar=0.0, op0=ALU.mult, op1=ALU.add,
                                         accum_out=lam[:, j:j + 1]).then_inc(trig_v, 1)
            dve.tensor_scalar(subln_s[:, 1:2], subln_s[:, 0:1], 1.0 - LAM_INIT, None, ALU.mult).then_inc(trig_v, 1)
            for q in range(2):
                dve.tensor_scalar(sink8[:, :, :].rearrange("p n (e q) -> p (n e) q", q=2)[:, :, q], sink_in[:, :],
                                  1.0 / SCALE_A, None, ALU.mult).then_inc(trig_v, 1)
            dve.wait_ge(trig_a, 1)
            c2 = cos[:, :, :].rearrange(flat)
            dve.tensor_tensor(c2, c2, c2, ALU.mult).then_inc(trig_v, 1)
            dve.wait_ge(trig_v, 15)
            dve.tensor_scalar(c2, c2, -2.0, 1.0, ALU.mult, ALU.add).then_inc(trig, 1)
            dve.wait_ge(trig_a, 2)
            dve.tensor_tensor(lam[:, 4:5], lam[:, 3:4], lam[:, 2:3], ALU.subtract).then_inc(trig_v, 1)
            dve.wait_ge(trig_v, 16)
            dve.tensor_scalar(lam[:, 5:6], lam[:, 4:5], LAM_INIT, None, ALU.subtract).then_inc(trig_v, 1)
            dve.wait_ge(trig_v, 17)

            for c in range(NC):
                turn_low(T_X0 + c, 4 * c, (X_hi, X_lo), 0)
            stat(0)
            for k in range(RING):
                split(0, k, WA)

            def slot_ab(k, diff=None, old=None, stick=None, first_stick=False):
                if stick is not None and k == 3:
                    j = stick - HEADS_A
                    dve.wait_ge(soft_done, j + 1)
                    if not first_stick:
                        dve.wait_ge(w_done, j)
                    dve.scalar_tensor_tensor(out=sp, in0=ps[5][:, 0:3 * P], scalar=0.0, in1=sp_a,
                                             op0=ALU.max, op1=ALU.add).then_inc(sp_part, 1)
                    dve.wait_ge(sp_part, j + 1)
                    diag = sp.rearrange("p (b c) -> p b c", b=3)[:, 0:3:2, :]
                    dve.tensor_tensor(diag, diag, strict01[:, None, :].to_broadcast([P, 2, P]),
                                      ALU.mult).then_inc(sp_ready, 1)
                if old is not None and k == 4:
                    dve.wait_ge(o_ready, old + 1)
                    if not isinstance(old, int) or old > 0:
                        dve.wait_ge(ors_ready, old)
                    for t in range(TB):
                        o_t = o_sb[:, t * P:(t + 1) * P]
                        last = dve.tensor_tensor_reduce(out=junk2[:, t, :], in0=o_t, in1=o_t, scale=1.0 / P, scalar=EPS,
                                                        op0=ALU.mult, op1=ALU.add, accum_out=oss[:, t:t + 1])
                    last.then_inc(oss_ready, 1)
                if stick is not None and k == 4:
                    dve.wait_ge(w_done, stick - HEADS_A + 1)
                    if not first_stick:
                        dve.wait_ge(wexp_done, stick - HEADS_A)
                    dve.tensor_tensor(wm, ps[6][:, 0:3 * P], strict[:, :], ALU.add).then_inc(wm_ready, 1)
                if diff is not None and k == 5:
                    dve.wait_ge(made, 1)
                    dve.wait_ge(scores_done, diff + 1)
                    for m in range(2):
                        for q, r in ((0, slice(0, P)), (1, slice(P, 3 * P))):
                            c = 2 * m + q
                            last = dve.tensor_tensor_reduce(out=sc[:, 0, m, r], in0=ps[5 + m][:, r], in1=full[:, r],
                                                            scale=1.0, scalar=-3.0e38, op0=ALU.add, op1=ALU.max,
                                                            accum_out=mx[:, c:c + 1])
                    last.then_inc(max_ready, 1)
                    dve.wait_ge(max_ready, diff + 1)
                    dve.tensor_scalar(negm, mx, -SCALE_A, None, ALU.mult).then_inc(negm_ready, 1)
                if old is not None and k == 5:
                    dve.wait_ge(ors_ready, old + 1)
                    if not isinstance(old, int) or old > 0:
                        dve.wait_ge(oT_done, old)
                    for t in range(TB):
                        last = dve.tensor_scalar(on_sb[:, t * P:(t + 1) * P], o_sb[:, t * P:(t + 1) * P],
                                                 ors[:, t:t + 1], None, ALU.mult)
                    last.then_inc(on_ready, 1)
                if diff is not None and k == 7:
                    dve.wait_ge(exp_done, diff + 1)
                    dve.reciprocal(rs, sums).then_inc(p_part, 1)
                    dve.wait_ge(p_part, 3 * diff + 1)
                    dve.tensor_scalar(rs[:, 2:4], rs[:, 2:4], lam[:, 5:6], None, ALU.mult).then_inc(p_part, 1)
                    if not isinstance(diff, int) or diff > 0:
                        dve.wait_ge(pT_done, diff)
                    dve.tensor_scalar(p_sb[:, 0:P], sc[:, 0, 0, 0:P], rs[:, 0:1], None, ALU.mult)
                    dve.tensor_scalar(p_sb[:, P:3 * P], sc[:, 0, 0, P:3 * P], rs[:, 1:2], None,
                                      ALU.mult).then_inc(p_part, 1)
                    dve.wait_ge(p_part, 3 * diff + 3)
                    dve.scalar_tensor_tensor(out=p_sb[:, 0:P], in0=sc[:, 0, 1, 0:P], scalar=rs[:, 2:3],
                                             in1=p_sb[:, 0:P], op0=ALU.mult, op1=ALU.add)
                    dve.scalar_tensor_tensor(out=p_sb[:, P:3 * P], in0=sc[:, 0, 1, P:3 * P], scalar=rs[:, 3:4],
                                             in1=p_sb[:, P:3 * P], op0=ALU.mult, op1=ALU.add).then_inc(p_ready, 1)
                if old is not None and k == 6:
                    dve.wait_ge(y_hi, old + 1)
                    dve.scalar_tensor_tensor(out=Y_lo[:, old, :], in0=ps[4][:, 0:S], scalar=subln_s[:, 1:2],
                                             in1=Y_hi[:, old, :].bitcast(F32), op0=ALU.mult,
                                             op1=ALU.subtract).then_inc(y_lo, 1)
                if stick is not None and k == 6:
                    dve.wait_ge(y_hi, stick + 1)
                    dve.tensor_tensor(Y_lo[:, stick, :], ps[7][:, 0:S], Y_hi[:, stick, :].bitcast(F32),
                                      ALU.subtract).then_inc(y_lo, 1)

            def unit_ab(U, wd_next=WA, **heads):
                for k in range(STEPS):
                    split(U, k + RING, WA if k + RING < STEPS else wd_next)
                    slot_ab(k, **heads)

            unit_ab(0)
            unit_ab(1, diff=0)
            unit_ab(2, diff=1, old=0)
            with dve.Fori(3, HEADS_A) as u:
                unit_ab(u, diff=u - 1, old=u - 2)
            unit_ab(8, diff=7, old=6)
            unit_ab(9, old=7, stick=8, first_stick=True)
            with dve.Fori(HEADS_A + 2, HEADS - 1) as u:
                unit_ab(u, stick=u - 1)
            unit_ab(HEADS - 1, wd_next=W, stick=HEADS - 2)

            def unit_out(U, par, n, before, heads=None, low=None, low_k=3):
                for k in range(STEPS):
                    split(U, k + RING, W)
                    if heads is not None:
                        slot_ab(k, **heads)
                    if low is not None and k == low_k:
                        turn_low(*low)
                add(U, par, n, before)

            Xs, Ys = (X_hi, X_lo), (Y_hi, Y_lo)
            for n in range(NC):
                unit_out(U_OAB + n, n % 2, n, n, heads=dict(stick=HEADS - 1) if n == 0 else None,
                         low=(T_X1 + n - 1, 4 * (n - 1), Xs, 1) if n > 0 else None)

            def mlp(s, U0, T_in, T_h, adds, norm, first, last, very_last):
                a = adds + NC * s
                for n in range(2 * NC):
                    U, par = U0 + 2 * NC * s + n, n % 2
                    for k in range(STEPS):
                        if not (very_last and n == 2 * NC - 1 and k + RING >= STEPS):
                            split(U, k + RING, W)
                        if n == 0 and first and k == 2:
                            stat(norm)
                        if n == 0 and first and k == 3:
                            turn_low(T_in + NC - 1, 4 * (NC - 1), Xs, norm)
                        if 1 <= n <= NC and k == 4:
                            turn_low(T_h + NC * s + n - 1, 4 * (n - 1), Ys)
                        if n > NC and last and k == 3:
                            turn_low(T_h + NC * SUPER + n - NC - 1, 4 * (n - NC - 1), Xs, norm + 1)
                    if n >= NC:
                        add(U, par, n - NC, a + n - NC)

            def mlps(U0, T_in, T_h, adds, norm, final):
                mlp(0, U0, T_in, T_h, adds, norm, True, False, False)
                with dve.Fori(1, SUPER - 1) as s:
                    mlp(s, U0, T_in, T_h, adds, norm, False, False, False)
                mlp(SUPER - 1, U0, T_in, T_h, adds, norm, False, not final, final)

            mlps(U_MLP0, T_X1, T_H0, NC, 1, False)

            def win_slot(k, g, old, last=False):
                def maxima(g, j):
                    n = PAIRS * g + j
                    late = not isinstance(n, int) or n >= 2
                    dve.wait_ge(c_scores, n + 1)
                    if late:
                        dve.wait_ge(c_pT, n - 1)
                    dve.memset(small[:, 60:61], 0.0)
                    for e in range(2):
                        for q, r in ((0, slice(0, P)), (1, slice(P, 3 * P))):
                            c = 2 * e + q
                            last_ = dve.tensor_tensor_reduce(out=sc[:, j % 2, e, r], in0=ps[6 + e][:, r],
                                                             in1=band[:, r], scale=1.0, scalar=-3.0e38,
                                                             op0=ALU.add, op1=ALU.max,
                                                             accum_out=mx_c[j % 2][:, c:c + 1])
                    last_.then_inc(c_max, 1)
                    dve.wait_ge(c_max, n + 1)
                    if late:
                        dve.wait_ge(c_sub, n - 1)
                    sink = sink8[:, n, :]
                    dve.tensor_tensor(M_c[j % 2], mx_c[j % 2], sink, ALU.max).then_inc(c_m, 1)
                    dve.wait_ge(c_m, n + 1)
                    if late:
                        dve.wait_ge(c_exp, n - 1)
                    dve.tensor_tensor(d_c[j % 2], sink, M_c[j % 2], ALU.subtract).then_inc(c_d, 1)

                def evac_pT(g, j):
                    n = PAIRS * g + j
                    dve.wait_ge(c_pT, n + 1)
                    if not isinstance(n, int) or n > 0:
                        dve.wait_ge(c_pv, n)
                    dve.tensor_copy(pT[:, 1, :], ps[5][:, 0:3 * P]).then_inc(c_pT_v, 1)

                def normalise(g, j):
                    n = PAIRS * g + j
                    dve.wait_ge(c_pv, n + 1)
                    o4 = ps[2][:, 0:4 * (DH + 1)].rearrange("p (e q c) -> p e q c", e=2, q=2)
                    dve.tensor_tensor(den.rearrange("p (e q) -> p e q", e=2), o4[:, :, :, DH],
                                      es_c[j % 2].rearrange("p (e q) -> p e q", e=2), ALU.add).then_inc(c_den, 1)
                    dve.wait_ge(c_den, 2 * n + 1)
                    dve.reciprocal(rden, den).then_inc(c_den, 1)
                    dve.wait_ge(c_den, 2 * n + 2)
                    if j == 0:
                        dve.wait_ge(turned, 2 * (T_C + g))
                    on = on_sb[:, :].rearrange("p (t c) -> p t c", t=TB)[:, :, j * P:(j + 1) * P]
                    dve.tensor_tensor(on.rearrange("p t (e d) -> p e t d", e=2), o4[:, :, :, 0:DH],
                                      rden.rearrange("p (e q) -> p e q", e=2)[:, :, :, None].to_broadcast([P, 2, 2, DH]),
                                      ALU.mult).then_inc(c_on, 1)

                if old is not None and k == 0:
                    normalise(old, 3)
                if old is not None and k == 1:
                    turn_low(T_C + old, 4 * old, Ys)
                if g is None:
                    return
                if k >= 3 and not (last and k > 5):
                    if k >= 4:
                        evac_pT(g, k - 4)
                    if k <= 6:
                        maxima(g, k - 3)
                    if k >= 5:
                        normalise(g, k - 5)
                if last and k == 5:
                    maxima(g, 3)
                    evac_pT(g, 2)
                    normalise(g, 1)
                    evac_pT(g, 3)
                    normalise(g, 2)
                    normalise(g, 3)
                    turn_low(T_C + g, 4 * g, Ys)

            def unit_c(U, hooks, first=False):
                for k in range(STEPS):
                    split(U, k + RING, W)
                    if first and k == 2:
                        stat(2)
                    if first and k == 3:
                        turn_low(T_X2 + NC - 1, 4 * (NC - 1), Xs, 2)
                    if hooks is not None:
                        win_slot(k, *hooks)

            unit_c(U_C, None, first=True)
            unit_c(U_C + 1, None)
            unit_c(U_C + 2, (0, None))
            with dve.Fori(1, GROUPS - 1) as g:
                unit_c(U_C + 2 + g, (g, g - 1))

            added = NC + NC * SUPER
            for n in range(NC):
                U = U_OC + n
                for k in range(STEPS):
                    split(U, k + RING, W)
                    if n == 0:
                        win_slot(k, GROUPS - 1, GROUPS - 2, last=True)
                    elif k == 3:
                        turn_low(T_X3 + n - 1, 4 * (n - 1), Xs, 3)
                add(U, n % 2, n, added + n)

            mlps(U_MLP1, T_X3, T_H1, added + NC, 3, True)
            stat(4)
            dve.wait_ge(stat_ready, 5)
            dve.wait_ge(w_landed[0], 16 * U_END + 16)
            for t in range(TB):
                dve.scalar_tensor_tensor(out=x_sb[:, t, :], in0=x_sb[:, t, :], scalar=rstd[:, 4, t:t + 1],
                                         in1=final_g, op0=ALU.mult, op1=ALU.mult).then_inc(fin, 1)

        @block.gpsimd
        def _(pool):
            zeros = [ident, band, full, strict]
            fills = [(t, 0.0) for t in zeros] + [(strict01, 1.0), (neg_tri, -1.0), (neg_one, -1.0), (half_pow, -0.5)]
            for t, v in fills:
                pool.memset(t[:, :], v).then_inc(made_part, 1)
            pool.memset(v_cur[:, :, :], 1.0).then_inc(made_part, 1)
            for f in range(DH // 2):
                freq = np.float32(10000.0) ** np.float32(-2.0 * f / DH)
                pool.memset(inv_freq[:, f:f + 1], float(freq)).then_inc(made_part, 1)
            pool.wait_ge(made_part, len(fills) + 1 + DH // 2)

            def keep(view, op, fill, down, along):
                return pool.affine_select(out=view, in_=view, compare_op=op, fill=fill, base=0,
                                          pattern=[[along, P]], channel_multiplier=down)

            for b in (0, 2):
                cols = slice(b * P, (b + 1) * P)
                keep(band[:, cols], ALU.is_ge, NEG, 1, -1)
                keep(full[:, cols], ALU.is_ge, NEG, 1, -1)
                keep(strict[:, cols], ALU.is_gt, NEG, -1, 1)
            keep(band[:, P:2 * P], ALU.is_gt, NEG, -1, 1)
            keep(strict01[:, :], ALU.is_gt, 0.0, -1, 1)
            keep(neg_tri[:, :], ALU.is_ge, 0.0, 1, -1)
            keep(ident[:, :], ALU.not_equal, 1.0, 1, -1).then_inc(made, 1)

            def rsqrt(i):
                pool.wait_ge(stat_v, 2 * i + 2)
                pool.tensor_tensor(rstd[:, i, :], ms[:, i, :], half_pow[:, :], ALU.pow).then_inc(stat_ready, 1)

            def rope(n, src, dst, tmp, groups):
                def halves(v, h):
                    return v.rearrange("p t (g h d) -> p t g h d", h=2, d=DH // 2)[:, :, :, h, :]

                def over(table, k):
                    return table[:, :, None, :].to_broadcast([P, TB, k, DH // 2])

                def blocks(v):
                    return v.rearrange("p t (g d) -> p t g d", d=DH // 2)

                pool.tensor_tensor(blocks(dst), blocks(src), over(cos, 2 * groups), ALU.mult).then_inc(rope_part, 1)
                pool.tensor_tensor(halves(tmp, 0), halves(src, 1), over(nsin, groups), ALU.mult).then_inc(rope_part, 1)
                pool.tensor_tensor(halves(tmp, 1), halves(src, 0), over(sin, groups), ALU.mult).then_inc(rope_part, 1)
                pool.wait_ge(rope_part, 3 * n + 3)
                pool.tensor_tensor(dst, dst, tmp, ALU.add).then_inc(rope_ready, 1)

            def narrow(t):
                return t[:, 0:TB * S].rearrange("p (t c) -> p t c", t=TB)

            def rope_head(h, par):
                pool.wait_ge(proj_ready, h + 1)
                if not isinstance(h, int) or h > 0:
                    pool.wait_ge(qkT_done, h)
                rope(h, qkv(par)[:, :, 0:S], narrow(rot), narrow(rot2), 4)

            def rsqrt_head(h):
                pool.wait_ge(oss_ready, h + 1)
                if not isinstance(h, int) or h > 0:
                    pool.wait_ge(on_ready, h)
                pool.tensor_tensor(ors, oss, half_pow[:, :], ALU.pow).then_inc(ors_ready, 1)

            rsqrt(0)
            pool.wait_ge(trig, 1)
            rope_head(0, 0)
            rope_head(1, 1)
            rsqrt_head(0)
            with pool.Fori(1, HEADS_A // 2) as i:
                rope_head(2 * i, 0)
                rsqrt_head(2 * i - 1)
                rope_head(2 * i + 1, 1)
                rsqrt_head(2 * i)
            rsqrt_head(HEADS_A - 1)
            rsqrt(1)

            def square(k, buf):
                pool.wait_ge(relu_ready, k + 1)
                pool.tensor_tensor(proj[:, buf, :], proj[:, buf, :], proj[:, buf, :], ALU.mult).then_inc(hid_ready, 1)

            with pool.Fori(0, NC * SUPER // 2) as i:
                square(2 * i, 0)
                square(2 * i + 1, 1)
            rsqrt(2)

            pool.wait_ge(proj_ready, HEADS + 1)
            wide_t = "p (t c) -> p t c"
            tmp_k = rot2[:, 0:TB * GROUPS * DH].rearrange(wide_t, t=TB)
            rope(HEADS_A, kv[:, :, 0:GROUPS * DH], krot[:, :, :], tmp_k, GROUPS)
            pool.wait_ge(rope_ready, HEADS_A + 1)

            def group(g):
                pool.wait_ge(proj_ready, HEADS + 2 + g)
                pool.wait_ge(qkT_done, HEADS + g)
                if not isinstance(g, int) or g > 0:
                    pool.wait_ge(c_pv, PAIRS * g)
                pool.tensor_copy(k_cur[:, :, :, :],
                                 krot[:, :, some(g * DH, DH)][:, :, None, :].to_broadcast([P, TB, 2, DH]))
                pool.tensor_copy(v_cur[:, :, 0:DH], kv[:, :, some(g * DH + GROUPS * DH, DH)])
                rope(HEADS_A + 1 + g, wide(0), rot[:, :].rearrange(wide_t, t=TB),
                     rot2[:, :].rearrange(wide_t, t=TB), 8)

            def shift(g, j):
                n = PAIRS * g + j
                pool.wait_ge(c_m, n + 1)
                for q, r in ((0, slice(0, P)), (1, slice(P, 3 * P))):
                    v = sc[:, j % 2, :, r]
                    m = M_c[j % 2].rearrange("p (e q) -> p e q", q=2)[:, :, q:q + 1]
                    last = pool.tensor_tensor(v, v, m.to_broadcast([P, 2, r.stop - r.start]), ALU.subtract)
                last.then_inc(c_sub, 1)

            def groups(g):
                group(g)
                for j in range(PAIRS):
                    shift(g, j)

            groups(0)
            with pool.Fori(1, GROUPS) as g:
                groups(g)
            rsqrt(3)
            with pool.Fori(NC * SUPER // 2, NC * SUPER) as i:
                square(2 * i, 0)
                square(2 * i + 1, 1)
            rsqrt(4)


def kernel(x, positions, norm_mix, norm_mlp, norm_final, w_in_ab, w_out_ab,
           lambda_q1, lambda_k1, lambda_q2, lambda_k2, diff_subln,
           w_in_c, w_out_c, sinks, w_up, w_down):
    import concourse.bacc as bacc
    from concourse.bass_utils import run_bass_kernel_spmd

    c = np.ascontiguousarray

    def loads(w):
        u, _, n = w.shape
        return c(w.reshape(u, LOADS, LK, P, n).transpose(0, 1, 3, 2, 4).reshape(u * LOADS, P, LK * n))

    def by_columns(w, n):
        return w.reshape(D, -1, n).transpose(1, 0, 2)

    w_in_ab, w_in_c, positions = np.asarray(w_in_ab)[0], np.asarray(w_in_c)[0], np.asarray(positions)
    x, w_up, w_down = np.asarray(x), np.asarray(w_up), np.asarray(w_down)
    ab = w_in_ab.reshape(D, 2, 3, HEADS_A, P).transpose(1, 3, 0, 2, 4).reshape(HEADS, D, WA)
    cw = np.concatenate([w_in_c[:, D:], w_in_c[:, :D]], axis=1)
    up = w_up.reshape(2, D, SUPER, NC, W).transpose(0, 2, 3, 1, 4)
    down = w_down.reshape(2, SUPER, D, NC, W).transpose(0, 1, 3, 2, 4)
    mlp = np.concatenate([up, down], axis=2).reshape(-1, D, W)
    norms = np.stack([norm_mix[0], norm_mlp[0], norm_mix[1], norm_mlp[1]])
    arrays = {
        "x": c(x[0]),
        "positions": c(positions[0].reshape(TB, P).T),
        "norm_t": c(norms.reshape(4, KT, P).transpose(2, 0, 1)),
        "norm_final": c(np.broadcast_to(np.asarray(norm_final), (P, D))),
        "w_ab": loads(ab),
        "w_oab": loads(by_columns(np.asarray(w_out_ab)[0], W)),
        "w_mlp": loads(mlp),
        "w_c": loads(by_columns(cw, W)),
        "w_oc": loads(by_columns(np.asarray(w_out_c)[0], W)),
        "lambdas": c(np.broadcast_to(np.concatenate([np.asarray(v)[0] for v in
                                                     (lambda_q1, lambda_k1, lambda_q2, lambda_k2)]), (P, 4 * DH))),
        "subln": c(np.asarray(diff_subln)[0].reshape(P, 1)),
        "sinks": c(np.broadcast_to(np.asarray(sinks)[0], (P, 2 * GROUPS * PAIRS))),
    }
    nc = bacc.Bacc("TRN2", target_bir_lowering=False, num_devices=1)
    args = [nc.dram_tensor(f"in_{n}", a.shape, mybir.dt.from_np(a.dtype), kind="ExternalInput").ap()
            for n, a in arrays.items()]
    args.append(nc.dram_tensor("out", (S, D), F32, kind="ExternalOutput").ap())
    trunk_kernel(nc, *args)
    r = run_bass_kernel_spmd(nc, [{f"in_{n}": a for n, a in arrays.items()}], core_ids=[0])
    return r.results[0]["out"].reshape(1, S, D)
```

```python
from contextlib import ExitStack

import numpy as np

import concourse.bass as bass
from concourse import mybir

F32 = mybir.dt.float32
F32R = mybir.dt.float32r
I32 = mybir.dt.int32
ALU = mybir.AluOpType
ACT = mybir.ActivationFunctionType
AX_X = mybir.AxisListType.X

P = 128
D = 2048
S = 256
TB = S // P
KT = D // P
STEPS = 8
SK = KT // STEPS
LOADS = 4
LK = KT // LOADS
RING = 4
W = 512
WA = 384
NC = D // W
D_FF = 4 * D
SUPER = D_FF // D
HEADS_A, HEADS_B = 8, 8
HEADS = HEADS_A + HEADS_B
GROUPS, PAIRS = 4, 4
DH = 64
EPS = 1e-6
NEG = -1e30
LAM_INIT = 0.8 - 0.6
SCALE_A = DH ** -0.5
SCALE_B = 128 ** -0.5

U_AB = 0
U_OAB = U_AB + HEADS
U_MLP0 = U_OAB + NC
U_C = U_MLP0 + 2 * NC * SUPER
U_OC = U_C + 1 + GROUPS
U_MLP1 = U_OC + NC
U_END = U_MLP1 + 2 * NC * SUPER

PAIR_ORDER = [(0, 0), (0, 1), (0, 2), (1, 0), (1, 1), (1, 2), (0, 3), (1, 3)]

T_X0 = 0
T_X1 = T_X0 + NC
T_H0 = T_X1 + NC
T_X2 = T_H0 + NC * SUPER
T_C = T_X2 + NC
T_X3 = T_C + GROUPS
T_H1 = T_X3 + NC


def some(start, size):
    return slice(start, start + size) if isinstance(start, int) else bass.ds(start, size)


def trunk_kernel(nc, x, positions, norm_t, norm_final, w_ab, w_oab, w_mlp, w_c, w_oc,
                 lambdas, subln, sinks, out):
    with ExitStack() as ctx:
        def sb(name, shape, dt=F32):
            return ctx.enter_context(nc.sbuf_tensor(name, shape, dt))

        def sem(name):
            return ctx.enter_context(nc.semaphore(name))

        x_sb = sb("x_sb", [P, TB, D])
        X_hi, X_lo = sb("X_hi", [P, KT, S], F32R), sb("X_lo", [P, KT, S], F32R)
        Y_hi, Y_lo = sb("Y_hi", [P, KT, S], F32R), sb("Y_lo", [P, KT, S], F32R)
        raw = sb("raw", [P, LOADS, LK * W])
        w_hi = sb("w_hi", [P, RING, SK * W], F32R)
        w_lo = sb("w_lo", [P, RING, SK * W], F32R)

        ident = sb("ident", [P, P])
        band = sb("band", [P, 3 * P])
        full = sb("full", [P, 3 * P])
        strict = sb("strict", [P, 3 * P])
        strict01 = sb("strict01", [P, P])
        neg_tri = sb("neg_tri", [P, P])
        neg_one = sb("neg_one", [P, P])
        norm_g = sb("norm_g", [P, 4, KT])
        lam_in = sb("lam_in", [P, 4, DH])
        lam = sb("lam", [P, 8])
        subln_s = sb("subln_s", [P, 2])
        sink_in = sb("sink_in", [P, 2 * GROUPS * PAIRS])
        sink8 = sb("sink8", [P, GROUPS * PAIRS, 4])
        half_pow = sb("half_pow", [P, 2])
        pos_i = sb("pos_i", [P, TB], I32)
        pos_f = sb("pos_f", [P, TB])
        inv_freq = sb("inv_freq", [P, DH // 2])
        ang = sb("ang", [P, TB, DH // 2])
        turns_i = sb("turns_i", [P, TB, DH // 2], I32)
        turns_f = sb("turns_f", [P, TB, DH // 2])
        cos = sb("cos", [P, TB, DH // 2])
        sin = sb("sin", [P, TB, DH // 2])
        nsin = sb("nsin", [P, TB, DH // 2])
        ss = sb("ss", [P, 5, TB, NC])
        ms = sb("ms", [P, 5, TB])
        rstd = sb("rstd", [P, 5, TB])
        junk = sb("junk", [P, TB, W])
        junk2 = sb("junk2", [P, TB, P])

        proj = sb("proj", [P, 2, TB * W])
        rot = sb("rot", [P, TB * W])
        rot2 = sb("rot2", [P, TB * W])
        qkT = sb("qkT", [P, 4 * S])
        kT = sb("kT", [P, S])
        sc = sb("sc", [P, 2, 2, 3 * P])
        small = sb("small", [P, 72])
        p_sb = sb("p_sb", [P, 3 * P])
        pT = sb("pT", [P, 2, 3 * P])
        o_sb = sb("o_sb", [P, TB * P])
        on_sb = sb("on_sb", [P, TB * W])
        kv = sb("kv", [P, TB, W])
        krot = sb("krot", [P, TB, GROUPS * DH])
        k_cur = sb("k_cur", [P, TB, 2, DH])
        v_cur = sb("v_cur", [P, TB, DH + 1])

        ps = [ctx.enter_context(nc.psum_tensor(f"bank{i}", [P, W], F32)) for i in range(8)]

        final_g = raw[:, 0, :]
        mx, negm, sums, rs = (small[:, 4 * i:4 * i + 4] for i in range(4))
        oss, ors = small[:, 16:18], small[:, 18:20]
        M_c = [small[:, 20 + 4 * i:24 + 4 * i] for i in range(2)]
        d_c = [small[:, 28 + 4 * i:32 + 4 * i] for i in range(2)]
        es_c = [small[:, 36 + 4 * i:40 + 4 * i] for i in range(PAIRS)]
        mx_c = [small[:, 52 + 4 * i:56 + 4 * i] for i in range(2)]
        den, rden, spare = small[:, 60:64], small[:, 64:68], small[:, 68:69]
        sp_a, sp, wm, wT = sc[:, 0, 0, :], sc[:, 0, 1, :], sc[:, 1, 0, :], sc[:, 1, 1, :]
        zm = p_sb[:, :]

        def qkv(par):
            return proj[:, par, 0:TB * WA].rearrange("p (t c) -> p t c", t=TB)

        def wide(par):
            return proj[:, par, :].rearrange("p (t c) -> p t c", t=TB)

        consts = sem("consts")
        smalls = sem("smalls")
        x_landed = [sem(f"x_landed{c}") for c in range(NC)]
        made_part, made = sem("made_part"), sem("made")
        trig_v, trig_a, trig = sem("trig_v"), sem("trig_a"), sem("trig")
        w_landed = [sem(f"w_landed{j}") for j in range(LOADS)]
        hi_ready, lo_ready = sem("hi_ready"), sem("lo_ready")
        steps_done = sem("steps_done")
        proj_ready = sem("proj_ready")
        x_added = sem("x_added")
        relu_ready = sem("relu_ready")
        hid_ready = sem("hid_ready")
        turned = sem("turned")
        turn_hi, turn_lo = sem("turn_hi"), sem("turn_lo")
        squared = sem("squared")
        stat_v, stat_ready = sem("stat_v"), sem("stat_ready")
        rope_cos = sem("rope_cos")
        rope_sin = sem("rope_sin")
        rope_ready = sem("rope_ready")
        v_ready, k_ready = sem("v_ready"), sem("k_ready")
        qkT_done, qkT_ready = sem("qkT_done"), sem("qkT_ready")
        scores_done = sem("scores_done")
        max_part, max_ready, negm_ready = sem("max_part"), sem("max_ready"), sem("negm_ready")
        exp_done = sem("exp_done")
        p_part, p_ready = sem("p_part"), sem("p_ready")
        pT_done, pT_ready = sem("pT_done"), sem("pT_ready")
        pv_done, o_ready = sem("pv_done"), sem("o_ready")
        oss_ready, ors_ready, on_ready = sem("oss_ready"), sem("ors_ready"), sem("on_ready")
        oT_done, y_hi, y_lo = sem("oT_done"), sem("y_hi"), sem("y_lo")
        soft_part, soft_done = sem("soft_part"), sem("soft_done")
        sp_part, sp_ready, zm_ready = sem("sp_part"), sem("sp_ready"), sem("zm_ready")
        w_done, wm_ready, wexp_done = sem("w_done"), sem("wm_ready"), sem("wexp_done")
        c_scores, c_max, c_m, c_d = sem("c_scores"), sem("c_max"), sem("c_m"), sem("c_d")
        c_sub, c_exp = sem("c_sub"), sem("c_exp")
        c_pT, c_pT_a, c_pT_v = sem("c_pT"), sem("c_pT_a"), sem("c_pT_v")
        c_pv, c_den, c_on = sem("c_pv"), sem("c_den"), sem("c_on")
        fin, stored = sem("fin"), sem("stored")

        block = ctx.enter_context(nc.Block())

        @block.sync
        def _(sp_):
            def load(src, first, U, wd, wait):
                for j in range(LOADS):
                    if wait:
                        sp_.wait_ge(lo_ready, 8 * U - 6 + 2 * j)
                    sp_.dma_start(raw[:, j, 0:LK * wd], src[first + j]).then_inc(w_landed[j], 16)

            sp_.dma_start(norm_g[:, :, :], norm_t).then_inc(consts, 16)
            for c in range(NC):
                sp_.dma_start(x_sb[:, :, c * W:(c + 1) * W],
                              x.rearrange("(t p) d -> p t d", p=P)[:, :, c * W:(c + 1) * W]).then_inc(x_landed[c], 16)
                if c > 0:
                    sp_.dma_start(raw[:, c - 1, 0:LK * WA], w_ab[c - 1]).then_inc(w_landed[c - 1], 16)
            sp_.dma_start(raw[:, NC - 1, 0:LK * WA], w_ab[NC - 1]).then_inc(w_landed[NC - 1], 16)
            sp_.dma_start(pos_i[:, :], positions).then_inc(smalls, 16)
            sp_.dma_start(lam_in[:, :, :].rearrange("p a b -> p (a b)"), lambdas).then_inc(smalls, 16)
            sp_.dma_start(subln_s[:, 0:1], subln).then_inc(smalls, 16)
            sp_.dma_start(sink_in[:, :], sinks).then_inc(smalls, 16)
            with sp_.Fori(1, HEADS) as i:
                load(w_ab, 4 * i, i, WA, True)
            with sp_.Fori(0, NC) as i:
                load(w_oab, 4 * i, U_OAB + i, W, True)
            with sp_.Fori(0, 2 * NC * SUPER) as i:
                load(w_mlp, 4 * i, U_MLP0 + i, W, True)
            with sp_.Fori(0, 1 + GROUPS) as i:
                load(w_c, 4 * i, U_C + i, W, True)
            with sp_.Fori(0, NC) as i:
                load(w_oc, 4 * i, U_OC + i, W, True)
            with sp_.Fori(0, 2 * NC * SUPER) as i:
                load(w_mlp, 4 * (2 * NC * SUPER) + 4 * i, U_MLP1 + i, W, True)
            sp_.wait_ge(lo_ready, 8 * U_END - 6)
            sp_.dma_start(final_g, norm_final).then_inc(w_landed[0], 16)
            for c in range(TB):
                sp_.wait_ge(fin, c + 1)
                sp_.dma_start(out.rearrange("(t p) d -> p t d", p=P)[:, c, :], x_sb[:, c, :]).then_inc(stored, 16)
            sp_.wait_ge(stored, 16 * TB)

        @block.tensor
        def _(pe):
            def step(U, k, par, A, wd, inputs=None, free=None, tiles=None):
                tiles = k if tiles is None else tiles
                pe.wait_ge(lo_ready, 8 * U + k + 1)
                if inputs is not None:
                    pe.wait_ge(inputs[0], inputs[1])
                if tiles == 0 and free is not None:
                    pe.wait_ge(free[0], free[1])
                A_hi, A_lo = A
                slot = k % RING
                for t in range(TB):
                    for q in range(SK):
                        kt = SK * tiles + q
                        rh = w_hi[:, slot, q * wd:(q + 1) * wd]
                        rl = w_lo[:, slot, q * wd:(q + 1) * wd]
                        o = ps[2 * par + t][:, 0:wd]
                        cols = slice(t * P, (t + 1) * P)
                        pe.matmul(o, A_lo[:, kt, cols], rh, start=(kt == 0), stop=False)
                        pe.matmul(o, A_hi[:, kt, cols], rl, start=False, stop=False)
                        last = pe.matmul(o, A_hi[:, kt, cols], rh, start=False, stop=(kt == KT - 1))
                last.then_inc(steps_done, 1)

            def turn(n, ready, value, src):
                pe.wait_ge(ready, value)
                if not isinstance(n, int) or n > 0:
                    pe.wait_ge(turn_lo, 2 * n)
                for b in range(2):
                    for q in range(2):
                        for t in range(TB):
                            kt = 2 * b + q
                            last = pe.transpose(ps[4 + b][:, q * S + t * P:q * S + (t + 1) * P],
                                                src[:, t, kt * P:(kt + 1) * P], ident[:, :])
                    last.then_inc(turned, 1)

            def diff_turn(h, first=False):
                pe.wait_ge(rope_ready, h + 1)
                if not first:
                    pe.wait_ge(y_lo, h - 1)
                for b, (t, c) in enumerate(((0, 0), (1, 0), (0, 1), (1, 1))):
                    last = pe.transpose(ps[4][:, b * P:(b + 1) * P],
                                        rot[:, t * S + c * P:t * S + (c + 1) * P], ident[:, :])
                last.then_inc(qkT_done, 1)

            def diff_scores(h, first=False):
                pe.wait_ge(qkT_ready, h + 1)
                if not first:
                    pe.wait_ge(max_ready, h)
                for q0, keys, at in ((0, P, 0), (P, S, P)):
                    for m in range(2):
                        r = slice(DH * m, DH * (m + 1))
                        last = pe.matmul(ps[5 + m][:, at:at + keys], qkT[r, q0:q0 + P], qkT[r, S:S + keys],
                                         start=True, stop=True)
                last.then_inc(scores_done, 1)

            def diff_pT(h, first=False):
                pe.wait_ge(p_ready, h + 1)
                if not first:
                    pe.wait_ge(o_ready, h)
                for b in range(3):
                    last = pe.transpose(ps[7][:, b * P:(b + 1) * P], p_sb[:, b * P:(b + 1) * P], ident[:, :])
                last.then_inc(pT_done, 1)

            def diff_pv(h, par):
                pe.wait_ge(pT_ready, h + 1)
                v = qkv(par)
                pe.matmul(ps[7][:, 0:P], pT[:, 0, 0:P], v[:, 0, S:WA], start=True, stop=True)
                pe.matmul(ps[7][:, P:S], pT[:, 0, P:S], v[:, 0, S:WA], start=True, stop=False)
                pe.matmul(ps[7][:, P:S], pT[:, 0, S:3 * P], v[:, 1, S:WA], start=False, stop=True).then_inc(pv_done, 1)

            def diff_oT(h):
                pe.wait_ge(on_ready, h + 1)
                pe.wait_ge(qkT_ready, h + 2)
                for t in range(TB):
                    last = pe.transpose(ps[4][:, t * P:(t + 1) * P], on_sb[:, t * P:(t + 1) * P], ident[:, :])
                last.then_inc(oT_done, 1)

            def stick_turn(h, par):
                pe.wait_ge(proj_ready, h + 1)
                pe.wait_ge(y_lo, h - 1)
                pe.wait_ge(qkT_ready, h)
                v = qkv(par)
                for b, (t, c) in enumerate(((0, 0), (1, 0), (0, 1), (1, 1))):
                    last = pe.transpose(ps[4][:, b * P:(b + 1) * P], v[:, t, c * P:(c + 1) * P], ident[:, :])
                last.then_inc(qkT_done, 1)

            def stick_z(h, first=False):
                pe.wait_ge(qkT_ready, h + 1)
                if first:
                    pe.wait_ge(max_ready, HEADS_A)
                else:
                    pe.wait_ge(wm_ready, h - HEADS_A)
                pe.matmul(ps[5][:, 0:S], qkT[:, S:S + P], qkT[:, 0:S], start=True, stop=True)
                pe.matmul(ps[5][:, S:3 * P], qkT[:, S + P:2 * S], qkT[:, P:S],
                          start=True, stop=True).then_inc(scores_done, 1)

            def stick_sum(h, first=False):
                pe.wait_ge(sp_ready, h - HEADS_A + 1)
                if not first:
                    pe.wait_ge(wm_ready, h - HEADS_A)
                pe.matmul(ps[6][:, 0:S], neg_tri[:, :], sp[:, 0:S], start=True, stop=False)
                pe.matmul(ps[6][:, P:S], neg_one[:, :], sp[:, S:3 * P], start=False, stop=True)
                pe.matmul(ps[6][:, S:3 * P], neg_tri[:, :], sp[:, S:3 * P],
                          start=True, stop=True).then_inc(w_done, 1)

            def stick_pv(h, par, first=False):
                pe.wait_ge(wexp_done, h - HEADS_A + 1)
                if first:
                    pe.wait_ge(o_ready, HEADS_A)
                else:
                    pe.wait_ge(y_lo, h)
                v = qkv(par)
                pe.matmul(ps[7][:, 0:S], v[:, 0, S:WA], wT[:, 0:S], start=True, stop=False)
                pe.matmul(ps[7][:, P:S], v[:, 1, S:WA], wT[:, S:3 * P], start=False, stop=True).then_inc(pv_done, 1)

            def win_turn(g):
                pe.wait_ge(rope_ready, HEADS_A + 2 + g)
                pe.wait_ge(k_ready, g + 1)
                pe.wait_ge(qkT_ready, HEADS + g)
                if not isinstance(g, int) or g > 0:
                    pe.wait_ge(c_max, PAIRS * g)
                for hp in range(PAIRS):
                    for t in range(TB):
                        pe.transpose(ps[(3, 7)[hp // 2]][:, (hp % 2) * S + t * P:(hp % 2) * S + (t + 1) * P],
                                     rot[:, t * W + hp * P:t * W + (hp + 1) * P], ident[:, :])
                for t in range(TB):
                    last = pe.transpose(ps[6][:, t * P:(t + 1) * P],
                                        k_cur[:, t].rearrange("p a b -> p (a b)"), ident[:, :])
                last.then_inc(qkT_done, 1)

            def win_scores(g, j):
                pe.wait_ge(qkT_ready, HEADS + 1 + g)
                if not (isinstance(g, int) and g == 0 and j == 0):
                    pe.wait_ge(c_max, PAIRS * g + j)
                for q0, keys, at in ((0, P, 0), (P, S, P)):
                    for e in range(2):
                        r = slice(DH * e, DH * (e + 1))
                        last = pe.matmul(ps[6 + e][:, at:at + keys], qkT[r, j * S + q0:j * S + q0 + P],
                                         kT[r, 0:keys], start=True, stop=True)
                last.then_inc(c_scores, 1)

            def win_pT(g, j):
                pe.wait_ge(c_exp, PAIRS * g + j + 1)
                if j == 0:
                    pe.wait_ge(turn_lo, 2 * (T_C + g))
                if not (isinstance(g, int) and g == 0 and j == 0):
                    pe.wait_ge(c_pT_a, PAIRS * g + j)
                    pe.wait_ge(c_pT_v, PAIRS * g + j)
                for e in range(2):
                    for b in range(3):
                        last = pe.transpose(ps[4 + e][:, b * P:(b + 1) * P],
                                            sc[:, j % 2, e, b * P:(b + 1) * P], ident[:, :])
                last.then_inc(c_pT, 1)

            def win_pv(g, j, bank=2):
                n = PAIRS * g + j
                if j == 0:
                    pe.wait_ge(v_ready, g + 1)
                    if bank == 6:
                        pe.wait_ge(c_max, PAIRS * g + PAIRS)
                pe.wait_ge(c_pT_a, n + 1)
                pe.wait_ge(c_pT_v, n + 1)
                if not (isinstance(n, int) and n == 0):
                    pe.wait_ge(c_on, n)
                C = DH + 1
                for e in range(2):
                    o0, o1 = (ps[bank][:, (2 * e + q) * C:(2 * e + q + 1) * C] for q in range(2))
                    pe.matmul(o0, pT[:, e, 0:P], v_cur[:, 0, :], start=True, stop=True)
                    pe.matmul(o1, pT[:, e, P:2 * P], v_cur[:, 0, :], start=True, stop=False)
                    last = pe.matmul(o1, pT[:, e, 2 * P:3 * P], v_cur[:, 1, :], start=False, stop=True)
                last.then_inc(c_pv, 1)

            def win_hooks(k, g, old):
                if old is not None and k == 0:
                    win_pT(old, 3)
                    win_pv(old, 2)
                if old is not None and k == 1:
                    win_pv(old, 3)
                if old is not None and k == 2:
                    turn(T_C + old, c_on, PAIRS * old + PAIRS, on_c)
                if k == 2:
                    win_turn(g)
                if k >= 5:
                    win_pT(g, k - 5)
                if 3 <= k <= 6:
                    win_scores(g, k - 3)
                if k >= 6:
                    win_pv(g, k - 6)

            def last_hooks(k):
                g = GROUPS - 1
                if k < STEPS:
                    if k <= 5:
                        win_hooks(k, g, g - 1)
                    if k == 6:
                        win_pT(g, 1)
                        win_scores(g, 3)
                    if k == 7:
                        win_pv(g, 0, 6)
                        win_pT(g, 2)
                if k == 8:
                    win_pv(g, 1, 6)
                    win_pT(g, 3)
                if k == 9:
                    win_pv(g, 2, 6)
                if k == 10:
                    win_pv(g, 3, 6)
                if k == 11:
                    turn(T_C + g, c_on, PAIRS * g + PAIRS, on_c)

            on_c = on_sb[:, :].rearrange("p (t c) -> p t c", t=TB)
            Xs, Ys = (X_hi, X_lo), (Y_hi, Y_lo)

            def turn_x(c):
                turn(T_X0 + c, x_landed[c], 16, x_sb[:, :, c * W:(c + 1) * W])

            pe.wait_ge(made, 1)
            turn_x(0)

            def unit_ab(U, par, diff=None, old=None, stick=None, first=False, first_stick=False):
                for k in range(STEPS):
                    inputs = (turn_lo, 2 * T_X0 + k + 1) if first else None
                    free = None if isinstance(U, int) and U < 2 else (proj_ready, U - 1)
                    step(U, k, par, Xs, WA, inputs, free)
                    if first and k in (0, 2, 4):
                        turn_x(k // 2 + 1)
                    hooks_ab(k, par, diff, old, stick, first_stick)

            def hooks_ab(k, par, diff, old, stick, first_stick):
                if old is not None and k == 0:
                    diff_pv(old, par)
                if stick is not None and k == 1:
                    stick_turn(stick, 1 - par)
                if stick is not None and k == 2:
                    stick_z(stick, first_stick)
                if diff is not None and k == 2:
                    diff_turn(diff, first=isinstance(diff, int) and diff < 2)
                if diff is not None and k == 3:
                    diff_scores(diff, first=isinstance(diff, int) and diff == 0)
                if stick is not None and k == 4:
                    stick_sum(stick, first_stick)
                if old is not None and k == 4:
                    diff_oT(old)
                if stick is not None and k == 6:
                    stick_pv(stick, 1 - par, first_stick)
                if diff is not None and k == 7:
                    diff_pT(diff, first=isinstance(diff, int) and diff == 0)

            unit_ab(0, 0, first=True)
            unit_ab(1, 1, diff=0)
            unit_ab(2, 0, diff=1, old=0)
            unit_ab(3, 1, diff=2, old=1)
            with pe.Fori(2, HEADS_A // 2) as i:
                unit_ab(2 * i, 0, diff=2 * i - 1, old=2 * i - 2)
                unit_ab(2 * i + 1, 1, diff=2 * i, old=2 * i - 1)
            unit_ab(8, 0, diff=7, old=6)
            unit_ab(9, 1, old=7, stick=8, first_stick=True)
            with pe.Fori(5, HEADS // 2) as i:
                unit_ab(2 * i, 0, stick=2 * i - 1)
                unit_ab(2 * i + 1, 1, stick=2 * i)

            for n in range(NC):
                U, par = U_OAB + n, n % 2
                for k in range(STEPS):
                    step(U, k, par, Ys, W, (y_lo, 2 * k + 2) if n == 0 else None,
                         (proj_ready, U - 1) if n < 2 else (x_added, n - 1))
                    if n == 0:
                        hooks_ab(k, par, None, None, HEADS - 1, False)
                    elif k == 2:
                        turn(T_X1 + n - 1, x_added, n, x_sb[:, :, (n - 1) * W:n * W])

            def mlp(s, U0, T_in, T_h, adds, relus, first, last):
                a, r = adds + NC * s, relus + NC * s
                for n in range(2 * NC):
                    U, par = U0 + 2 * NC * s + n, n % 2
                    up = n < NC
                    for k in range(STEPS):
                        inputs = None
                        if n == 0 and first:
                            inputs = (turn_lo, 2 * T_in + k + 1)
                        if n == NC:
                            inputs = (turn_lo, 2 * (T_h + NC * s) + k + 1)
                        if n in (0, 1):
                            free = (x_added, a - 1 + n)
                        elif n < NC + 2:
                            free = (relu_ready, r + n - 1)
                        else:
                            free = (x_added, a + n - NC - 1)
                        step(U, k, par, Xs if up else Ys, W, inputs, free)
                        if n == 0 and first and k == 2:
                            turn(T_in + NC - 1, x_added, a, x_sb[:, :, (NC - 1) * W:NC * W])
                        if 1 <= n <= NC and k == 3:
                            turn(T_h + NC * s + n - 1, hid_ready, r + n, wide((n - 1) % 2))
                        if n > NC and last and k == 2:
                            turn(T_h + NC * SUPER + n - NC - 1, x_added, a + n - NC,
                                 x_sb[:, :, (n - NC - 1) * W:(n - NC) * W])

            def mlps(U0, T_in, T_h, adds, relus, turns_after):
                mlp(0, U0, T_in, T_h, adds, relus, True, False)
                with pe.Fori(1, SUPER - 1) as s:
                    mlp(s, U0, T_in, T_h, adds, relus, False, False)
                mlp(SUPER - 1, U0, T_in, T_h, adds, relus, False, turns_after)

            mlps(U_MLP0, T_X1, T_H0, NC, 0, True)

            def unit_c(U, hooks, free, first=False):
                for k in range(STEPS):
                    step(U, k, 0, Xs, W, (turn_lo, 2 * T_X2 + k + 1) if first else None, free)
                    if first and k == 2:
                        turn(T_X2 + NC - 1, x_added, NC + NC * SUPER, x_sb[:, :, (NC - 1) * W:NC * W])
                    if hooks is not None:
                        win_hooks(k, *hooks)

            unit_c(U_C, None, (x_added, NC + NC * SUPER - 1), first=True)
            unit_c(U_C + 1, None, (proj_ready, HEADS + 1))
            unit_c(U_C + 2, (0, None), (proj_ready, HEADS + 2))
            with pe.Fori(1, GROUPS - 1) as g:
                unit_c(U_C + 2 + g, (g, g - 1), (proj_ready, HEADS + 2 + g))

            added = NC + NC * SUPER
            for k in range(2 * STEPS):
                n, tiles = PAIR_ORDER[k // 2][0], 2 * PAIR_ORDER[k // 2][1] + k % 2
                if tiles == 0 and n == 1:
                    pe.wait_ge(qkT_ready, HEADS + GROUPS)
                free = ((proj_ready, HEADS + 1 + GROUPS), (c_on, (GROUPS - 1) * PAIRS))[n]
                step(U_OC, k, n, Ys, W, (turn_lo, 2 * T_C + tiles + 1), free, tiles)
                last_hooks(k)
            for n in range(2, NC):
                for k in range(STEPS):
                    step(U_OC + n, k, n % 2, Ys, W, None, (x_added, added + n - 1))
                    if k in ((0, 2) if n == 2 else (2,)):
                        c = n - 1 if k == 2 else 0
                        turn(T_X3 + c, x_added, added + c + 1, x_sb[:, :, c * W:(c + 1) * W])

            mlps(U_MLP1, T_X3, T_H1, added + NC, NC * SUPER, False)

        @block.scalar
        def _(act):
            def split(U, k, wd):
                if k >= STEPS:
                    U, k = U + 1, k - STEPS
                if k % 2 == 0:
                    act.wait_ge(w_landed[k // 2], 16 * U + 16)
                if not isinstance(U, int) or 8 * U + k >= RING:
                    act.wait_ge(steps_done, 8 * U + k - RING + 1)
                act.activation(w_hi[:, k % RING, 0:SK * wd],
                               raw[:, k // 2, (k % 2) * SK * wd:(k % 2 + 1) * SK * wd],
                               ACT.Copy).then_inc(hi_ready, 1)

            def turn_high(n, kt0, A_hi, g=None):
                for b in range(2):
                    act.wait_ge(turned, 2 * n + b + 1)
                    if g is None:
                        last = act.activation(A_hi[:, some(kt0 + 2 * b, 2), :],
                                              ps[4 + b][:, :].rearrange("p (a b) -> p a b", a=2), ACT.Copy)
                    else:
                        for q in range(2):
                            kt = kt0 + 2 * b + q
                            last = act.activation(A_hi[:, kt, :], ps[4 + b][:, q * S:(q + 1) * S], ACT.Copy,
                                                  scale=norm_g[:, g, kt:kt + 1])
                    last.then_inc(turn_hi, 1)

            def squares(i, c, ready, value):
                act.wait_ge(ready, value)
                if i or c:
                    act.wait_ge(squared, NC * i + c)
                for t in range(TB):
                    last = act.activation(junk[:, t, :], x_sb[:, t, c * W:(c + 1) * W], ACT.Square,
                                          accum_out=ss[:, i, t, c:c + 1])
                last.then_inc(squared, 1)

            def evacuate(U, par, dst, wd, func, i, done):
                act.wait_ge(steps_done, 8 * U + 8)
                for t in range(TB):
                    last = act.activation(dst[:, t, 0:wd], ps[2 * par + t][:, 0:wd], func,
                                          scale=rstd[:, i, t:t + 1])
                last.then_inc(done, 1)

            act.wait_ge(consts, 16)
            turn_high(T_X0, 0, X_hi, 0)
            for k in range(RING):
                split(0, k, WA)

            def angles():
                act.wait_ge(trig_v, 9)
                act.activation(cos[:, :, :], ang[:, :, :], ACT.Sin, scale=0.5)
                act.activation(sin[:, :, :], ang[:, :, :], ACT.Sin)
                act.activation(nsin[:, :, :], ang[:, :, :], ACT.Sin, scale=-1.0).then_inc(trig_a, 1)
                act.preload_act_table_set("natural_log_exp_and_others")
                act.wait_ge(trig_v, 12)
                act.activation(lam[:, 2:4], lam[:, 0:2], ACT.Exp).then_inc(trig_a, 1)

            def slot_ab(k, diff=None, old=None, stick=None, first_stick=False):
                if old is not None and k == 0:
                    act.wait_ge(pv_done, old + 1)
                    if not isinstance(old, int) or old > 0:
                        act.wait_ge(on_ready, old)
                    act.activation(o_sb[:, :], ps[7][:, 0:S], ACT.Copy).then_inc(o_ready, 1)
                if diff is not None and k == 2:
                    act.wait_ge(qkT_done, diff + 1)
                    if not isinstance(diff, int) or diff > 0:
                        act.wait_ge(scores_done, diff)
                    act.activation(qkT[:, 0:2 * S], ps[4][:, :], ACT.Copy).then_inc(qkT_ready, 1)
                if diff is not None and k == 4:
                    act.wait_ge(negm_ready, diff + 1)
                    for m in range(2):
                        for q, r in ((0, slice(0, P)), (1, slice(P, 3 * P))):
                            c = 2 * m + q
                            last = act.activation(sc[:, 0, m, r], sc[:, 0, m, r], ACT.Exp, bias=negm[:, c:c + 1],
                                                  scale=SCALE_A, accum_out=sums[:, c:c + 1])
                    last.then_inc(exp_done, 1)
                if stick is not None and k == 1:
                    act.wait_ge(qkT_done, stick + 1)
                    act.wait_ge(scores_done, stick)
                    act.activation(qkT[:, 0:S], ps[4][:, 0:S], ACT.Copy, scale=SCALE_B)
                    act.activation(qkT[:, S:2 * S], ps[4][:, S:2 * S], ACT.Copy).then_inc(qkT_ready, 1)
                if stick is not None and k == 2:
                    j = stick - HEADS_A
                    act.wait_ge(scores_done, stick + 1)
                    if first_stick:
                        act.wait_ge(p_ready, HEADS_A)
                    else:
                        act.wait_ge(sp_ready, j)
                    act.activation(sp_a, ps[5][:, 0:3 * P], ACT.Abs).then_inc(soft_part, 1)
                    act.wait_ge(soft_part, 2 * j + 1)
                    act.activation(sp_a, sp_a, ACT.Exp, scale=-1.0).then_inc(soft_part, 1)
                    act.wait_ge(soft_part, 2 * j + 2)
                    act.activation(sp_a, sp_a, ACT.Ln, bias=1.0).then_inc(soft_done, 1)
                if stick is not None and k == 4:
                    act.wait_ge(wm_ready, stick - HEADS_A + 1)
                    act.wait_ge(pv_done, stick)
                    act.activation(wT, wm, ACT.Exp).then_inc(wexp_done, 1)
                if old is not None and k == 4:
                    act.wait_ge(oT_done, old + 1)
                    act.activation(Y_hi[:, old, :], ps[4][:, 0:S], ACT.Copy, scale=subln_s[:, 1:2]).then_inc(y_hi, 1)
                if stick is not None and k == 6:
                    act.wait_ge(pv_done, stick + 1)
                    act.activation(Y_hi[:, stick, :], ps[7][:, 0:S], ACT.Copy).then_inc(y_hi, 1)
                if diff is not None and k == 7:
                    act.wait_ge(pT_done, diff + 1)
                    act.activation(pT[:, 0, :], ps[7][:, 0:3 * P], ACT.Copy).then_inc(pT_ready, 1)

            def unit_ab(U, par, wd_next=WA, **heads):
                for k in range(STEPS):
                    split(U, k + RING, WA if k + RING < STEPS else wd_next)
                    if isinstance(U, int) and U == 0:
                        if k in (0, 2, 4):
                            turn_high(T_X0 + k // 2 + 1, 4 * (k // 2 + 1), X_hi, 0)
                        if k == 1:
                            angles()
                        if k >= 4:
                            squares(0, k - 4, x_landed[k - 4], 16)
                    slot_ab(k, **heads)
                if isinstance(U, int) and U == 0:
                    act.wait_ge(stat_ready, 1)
                if not isinstance(U, int) or U >= 2:
                    act.wait_ge(pv_done, U - 1)
                evacuate(U, par, qkv(par), WA, ACT.Copy, 0, proj_ready)

            unit_ab(0, 0)
            unit_ab(1, 1, diff=0)
            unit_ab(2, 0, diff=1, old=0)
            unit_ab(3, 1, diff=2, old=1)
            with act.Fori(2, HEADS_A // 2) as i:
                unit_ab(2 * i, 0, diff=2 * i - 1, old=2 * i - 2)
                unit_ab(2 * i + 1, 1, diff=2 * i, old=2 * i - 1)
            unit_ab(8, 0, diff=7, old=6)
            unit_ab(9, 1, old=7, stick=8, first_stick=True)
            with act.Fori(5, HEADS // 2 - 1) as i:
                unit_ab(2 * i, 0, stick=2 * i - 1)
                unit_ab(2 * i + 1, 1, stick=2 * i)
            unit_ab(14, 0, stick=13)
            unit_ab(15, 1, wd_next=W, stick=14)

            for n in range(NC):
                U = U_OAB + n
                for k in range(STEPS):
                    split(U, k + RING, W)
                    if n == 0:
                        slot_ab(k, stick=HEADS - 1)
                    if n > 0 and k == 1:
                        squares(1, n - 1, x_added, n)
                    if n > 0 and k == 3:
                        turn_high(T_X1 + n - 1, 4 * (n - 1), X_hi, 1)

            def mlp(s, U0, T_in, T_h, adds, relus, norm, first, last, very_last):
                a, r = adds + NC * s, relus + NC * s
                for n in range(2 * NC):
                    U, par = U0 + 2 * NC * s + n, n % 2
                    for k in range(STEPS):
                        if not (very_last and n == 2 * NC - 1 and k + RING >= STEPS):
                            split(U, k + RING, W)
                        if n == 0 and first and k == 1:
                            squares(norm, NC - 1, x_added, a)
                        if n == 0 and first and k == 3:
                            turn_high(T_in + NC - 1, 4 * (NC - 1), X_hi, norm)
                        if 1 <= n <= NC and k == 4:
                            turn_high(T_h + NC * s + n - 1, 4 * (n - 1), Y_hi)
                        if n > NC and (last or very_last) and k == 1:
                            squares(norm + 1, n - NC - 1, x_added, a + n - NC)
                        if n > NC and last and k == 3:
                            turn_high(T_h + NC * SUPER + n - NC - 1, 4 * (n - NC - 1), X_hi, norm + 1)
                    if n < NC:
                        if n == 0 and first:
                            act.wait_ge(stat_ready, norm + 1)
                        act.wait_ge(turned, 2 * (T_h + NC * s + n - 1))
                        evacuate(U, par, wide(n % 2), W, ACT.Relu, norm, relu_ready)

            def mlps(U0, T_in, T_h, adds, relus, norm, final):
                mlp(0, U0, T_in, T_h, adds, relus, norm, True, False, False)
                with act.Fori(1, SUPER - 1) as s:
                    mlp(s, U0, T_in, T_h, adds, relus, norm, False, False, False)
                mlp(SUPER - 1, U0, T_in, T_h, adds, relus, norm, False, not final, final)

            mlps(U_MLP0, T_X1, T_H0, NC, 0, 1, False)

            def evac_pT(g, j):
                n = PAIRS * g + j
                act.wait_ge(c_pT, n + 1)
                if not (isinstance(n, int) and n == 0):
                    act.wait_ge(c_pv, n)
                act.activation(pT[:, 0, :], ps[4][:, 0:3 * P], ACT.Copy).then_inc(c_pT_a, 1)

            def exps(g, j):
                n = PAIRS * g + j
                both = sc[:, j % 2].rearrange("p a b -> p (a b)")
                act.wait_ge(c_sub, n + 1)
                act.activation(both, both, ACT.Exp, scale=SCALE_A)
                act.wait_ge(c_d, n + 1)
                if not isinstance(g, int) or g > 0:
                    act.wait_ge(c_den, 2 * n - 7)
                act.activation(es_c[j], d_c[j % 2], ACT.Exp, scale=SCALE_A).then_inc(c_exp, 1)

            def win_slot(k, g, old):
                if old is not None and k == 0:
                    evac_pT(old, 3)
                if old is not None and k == 2:
                    turn_high(T_C + old, 4 * old, Y_hi)
                if k == 2:
                    act.wait_ge(qkT_done, HEADS + 1 + g)
                    act.activation(kT[:, :], ps[6][:, 0:S], ACT.Copy)
                    for b in range(2):
                        last_ = act.activation(qkT[:, b * 2 * S:(b + 1) * 2 * S], ps[(3, 7)[b]][:, :], ACT.Copy)
                    last_.then_inc(qkT_ready, 1)
                if k >= 5:
                    evac_pT(g, k - 5)
                if k >= 4:
                    exps(g, k - 4)

            def unit_c(U, dst, hooks, first=False):
                for k in range(STEPS):
                    split(U, k + RING, W)
                    if first and k == 1:
                        squares(2, NC - 1, x_added, NC + NC * SUPER)
                    if first and k == 3:
                        turn_high(T_X2 + NC - 1, 4 * (NC - 1), X_hi, 2)
                    if hooks is not None:
                        win_slot(k, *hooks)
                if first:
                    act.wait_ge(stat_ready, 3)
                else:
                    act.wait_ge(rope_ready, U - U_C + HEADS_A)
                evacuate(U, 0, dst, W, ACT.Copy, 2, proj_ready)

            unit_c(U_C, kv[:, :, :], None, first=True)
            unit_c(U_C + 1, wide(0), None)
            unit_c(U_C + 2, wide(0), (0, None))
            with act.Fori(1, GROUPS - 1) as g:
                unit_c(U_C + 2 + g, wide(0), (g, g - 1))

            g = GROUPS - 1
            for n in range(NC):
                U = U_OC + n
                for k in range(STEPS):
                    split(U, k + RING, W)
                    if n == 0:
                        win_slot(k, g, g - 1)
                    if n == 1 and k == 0:
                        evac_pT(g, 3)
                    if n == 1 and k == 3:
                        turn_high(T_C + g, 4 * g, Y_hi)
                    if n >= 2:
                        for c in ((0, 1) if n == 2 else (2,)):
                            if k == (0, 2, 2)[c]:
                                squares(3, c, x_added, NC + NC * SUPER + c + 1)
                                turn_high(T_X3 + c, 4 * c, X_hi, 3)

            mlps(U_MLP1, T_X3, T_H1, 2 * NC + NC * SUPER, NC * SUPER, 3, True)
            squares(4, NC - 1, x_added, 2 * NC + 2 * NC * SUPER)

        @block.vector
        def _(dve):
            def split(U, k, wd):
                if k >= STEPS:
                    U, k = U + 1, k - STEPS
                dve.wait_ge(hi_ready, 8 * U + k + 1)
                dve.tensor_tensor(w_lo[:, k % RING, 0:SK * wd],
                                  raw[:, k // 2, (k % 2) * SK * wd:(k % 2 + 1) * SK * wd],
                                  w_hi[:, k % RING, 0:SK * wd].bitcast(F32), ALU.subtract).then_inc(lo_ready, 1)

            def turn_low(n, kt0, A, g=None):
                A_hi, A_lo = A
                for b in range(2):
                    dve.wait_ge(turn_hi, 2 * n + b + 1)
                    if g is None:
                        at = some(kt0 + 2 * b, 2)
                        last = dve.tensor_tensor(A_lo[:, at, :], ps[4 + b][:, :].rearrange("p (a b) -> p a b", a=2),
                                                 A_hi[:, at, :].bitcast(F32), ALU.subtract)
                    else:
                        for q in range(2):
                            kt = kt0 + 2 * b + q
                            last = dve.scalar_tensor_tensor(out=A_lo[:, kt, :], in0=ps[4 + b][:, q * S:(q + 1) * S],
                                                            scalar=norm_g[:, g, kt:kt + 1],
                                                            in1=A_hi[:, kt, :].bitcast(F32),
                                                            op0=ALU.mult, op1=ALU.subtract)
                    last.then_inc(turn_lo, 1)

            def add(U, par, n, before, steps=STEPS):
                dve.wait_ge(steps_done, 8 * U + steps)
                if not isinstance(before, int) or before >= NC:
                    dve.wait_ge(x_added, before - NC + 1)
                for t in range(TB):
                    xc = x_sb[:, t, n * W:(n + 1) * W]
                    last = dve.tensor_tensor(xc, ps[2 * par + t][:, :], xc, ALU.add)
                last.then_inc(x_added, 1)

            def stat(i):
                dve.wait_ge(squared, NC * (i + 1))
                dve.tensor_reduce(ms[:, i, :], ss[:, i, :, :], AX_X, ALU.add).then_inc(stat_v, 1)
                dve.wait_ge(stat_v, 2 * i + 1)
                dve.tensor_scalar(ms[:, i, :], ms[:, i, :], 1.0 / D, EPS, ALU.mult, ALU.add).then_inc(stat_v, 1)

            dve.wait_ge(consts, 16)
            turn_low(T_X0, 0, (X_hi, X_lo), 0)
            for k in range(RING):
                split(0, k, WA)

            def angles():
                dve.wait_ge(made, 1)
                dve.wait_ge(smalls, 64)
                dve.tensor_copy(pos_f[:, :], pos_i[:, :]).then_inc(trig_v, 1)
                dve.wait_ge(trig_v, 1)
                for t in range(TB):
                    dve.tensor_scalar(ang[:, t, :], inv_freq[:, :], pos_f[:, t:t + 1], None, ALU.mult).then_inc(trig_v, 1)
                dve.wait_ge(trig_v, 3)
                flat = "p t c -> p (t c)"
                a2, i2, f2 = (v[:, :, :].rearrange(flat) for v in (ang, turns_i, turns_f))
                dve.tensor_scalar(i2, a2, 1.0 / (2.0 * np.pi), None, ALU.mult).then_inc(trig_v, 1)
                dve.wait_ge(trig_v, 4)
                dve.tensor_copy(f2, i2).then_inc(trig_v, 1)
                parts = [6.28125]
                parts.append(float(np.float32(np.round((2 * np.pi - parts[0]) * 2 ** 21) / 2 ** 21)))
                parts.append(float(np.float32(2 * np.pi - parts[0] - parts[1])))
                for j, part in enumerate(parts):
                    dve.wait_ge(trig_v, 5 + j)
                    dve.scalar_tensor_tensor(out=a2, in0=f2, scalar=-part, in1=a2,
                                             op0=ALU.mult, op1=ALU.add).then_inc(trig_v, 1)
                dve.wait_ge(trig_v, 8)
                lim = 3.1415925
                dve.tensor_scalar(a2, a2, -lim, lim, ALU.max, ALU.min).then_inc(trig_v, 1)
                for j in range(2):
                    dve.tensor_tensor_reduce(out=junk2[:, j, 0:DH], in0=lam_in[:, 2 * j, :], in1=lam_in[:, 2 * j + 1, :],
                                             scale=1.0, scalar=0.0, op0=ALU.mult, op1=ALU.add,
                                             accum_out=lam[:, j:j + 1]).then_inc(trig_v, 1)
                dve.tensor_scalar(subln_s[:, 1:2], subln_s[:, 0:1], 1.0 - LAM_INIT, None, ALU.mult).then_inc(trig_v, 1)
                for q in range(2):
                    dve.tensor_scalar(sink8[:, :, :].rearrange("p n (e q) -> p (n e) q", q=2)[:, :, q], sink_in[:, :],
                                      1.0 / SCALE_A, None, ALU.mult).then_inc(trig_v, 1)
                dve.wait_ge(trig_a, 1)
                c2 = cos[:, :, :].rearrange(flat)
                dve.tensor_tensor(c2, c2, c2, ALU.mult).then_inc(trig_v, 1)
                dve.wait_ge(trig_v, 15)
                dve.tensor_scalar(c2, c2, -2.0, 1.0, ALU.mult, ALU.add).then_inc(trig, 1)
                dve.wait_ge(trig_a, 2)
                dve.tensor_tensor(lam[:, 4:5], lam[:, 3:4], lam[:, 2:3], ALU.subtract).then_inc(trig_v, 1)
                dve.wait_ge(trig_v, 16)
                dve.tensor_scalar(lam[:, 5:6], lam[:, 4:5], LAM_INIT, None, ALU.subtract).then_inc(trig_v, 1)
                dve.wait_ge(trig_v, 17)

            def rope_x(n, src, dst, groups):
                blocks = "p t (g d) -> p t g d"
                dve.tensor_tensor(dst.rearrange(blocks, d=DH // 2), src.rearrange(blocks, d=DH // 2),
                                  cos[:, :, None, :].to_broadcast([P, TB, 2 * groups, DH // 2]),
                                  ALU.mult).then_inc(rope_cos, 1)

            def rope_sum(n, dst, tmp):
                dve.wait_ge(rope_cos, n + 1)
                dve.wait_ge(rope_sin, 2 * n + 2)
                dve.tensor_tensor(dst, dst, tmp, ALU.add).then_inc(rope_ready, 1)

            def rope_head(k, h, par):
                rot_h, rot2_h = (v[:, 0:TB * S].rearrange("p (t c) -> p t c", t=TB) for v in (rot, rot2))
                if k == 0:
                    dve.wait_ge(proj_ready, h + 1)
                    if not isinstance(h, int) or h > 0:
                        dve.wait_ge(qkT_done, h)
                    rope_x(h, qkv(par)[:, :, 0:S], rot_h, 4)
                if k == 1:
                    rope_sum(h, rot_h, rot2_h)

            def slot_ab(k, par, diff=None, old=None, stick=None, first_stick=False):
                if diff is not None and k <= 1:
                    rope_head(k, diff, 1 - par)
                if stick is not None and k == 2:
                    j = stick - HEADS_A
                    dve.wait_ge(soft_done, j + 1)
                    if not first_stick:
                        dve.wait_ge(w_done, j)
                    dve.scalar_tensor_tensor(out=sp, in0=ps[5][:, 0:3 * P], scalar=0.0, in1=sp_a,
                                             op0=ALU.max, op1=ALU.add).then_inc(sp_part, 1)
                    dve.wait_ge(sp_part, j + 1)
                    diag = sp.rearrange("p (b c) -> p b c", b=3)[:, 0:3:2, :]
                    dve.tensor_tensor(diag, diag, strict01[:, None, :].to_broadcast([P, 2, P]),
                                      ALU.mult).then_inc(sp_ready, 1)
                    if first_stick:
                        dve.wait_ge(pT_done, HEADS_A)
                    else:
                        dve.wait_ge(wm_ready, j)
                    dve.tensor_tensor(zm, ps[5][:, 0:3 * P], strict[:, :], ALU.add).then_inc(zm_ready, 1)
                if old is not None and k == 0:
                    dve.wait_ge(o_ready, old + 1)
                    if not isinstance(old, int) or old > 0:
                        dve.wait_ge(ors_ready, old)
                    for t in range(TB):
                        o_t = o_sb[:, t * P:(t + 1) * P]
                        last = dve.tensor_tensor_reduce(out=junk2[:, t, :], in0=o_t, in1=o_t, scale=1.0 / P, scalar=EPS,
                                                        op0=ALU.mult, op1=ALU.add, accum_out=oss[:, t:t + 1])
                    last.then_inc(oss_ready, 1)
                if stick is not None and k == 4:
                    dve.wait_ge(w_done, stick - HEADS_A + 1)
                    if not first_stick:
                        dve.wait_ge(wexp_done, stick - HEADS_A)
                    dve.wait_ge(zm_ready, stick - HEADS_A + 1)
                    dve.tensor_tensor(wm, ps[6][:, 0:3 * P], zm, ALU.add).then_inc(wm_ready, 1)
                if diff is not None and k == 3:
                    dve.wait_ge(made, 1)
                    dve.wait_ge(scores_done, diff + 1)
                    for m in range(2):
                        for q, r in ((0, slice(0, P)), (1, slice(P, 3 * P))):
                            c = 2 * m + q
                            last = dve.tensor_tensor_reduce(out=sc[:, 0, m, r], in0=ps[5 + m][:, r], in1=full[:, r],
                                                            scale=1.0, scalar=-3.0e38, op0=ALU.add, op1=ALU.max,
                                                            accum_out=mx[:, c:c + 1])
                    last.then_inc(max_ready, 1)
                    dve.wait_ge(max_ready, diff + 1)
                    dve.tensor_scalar(negm, mx, -SCALE_A, None, ALU.mult).then_inc(negm_ready, 1)
                if old is not None and k == 2:
                    dve.wait_ge(ors_ready, old + 1)
                    if not isinstance(old, int) or old > 0:
                        dve.wait_ge(oT_done, old)
                    for t in range(TB):
                        last = dve.tensor_scalar(on_sb[:, t * P:(t + 1) * P], o_sb[:, t * P:(t + 1) * P],
                                                 ors[:, t:t + 1], None, ALU.mult)
                    last.then_inc(on_ready, 1)
                if diff is not None and k == 5:
                    dve.wait_ge(exp_done, diff + 1)
                    dve.reciprocal(rs, sums).then_inc(p_part, 1)
                    dve.wait_ge(p_part, 3 * diff + 1)
                    dve.tensor_scalar(rs[:, 2:4], rs[:, 2:4], lam[:, 5:6], None, ALU.mult).then_inc(p_part, 1)
                    if not isinstance(diff, int) or diff > 0:
                        dve.wait_ge(pT_done, diff)
                    dve.tensor_scalar(p_sb[:, 0:P], sc[:, 0, 0, 0:P], rs[:, 0:1], None, ALU.mult)
                    dve.tensor_scalar(p_sb[:, P:3 * P], sc[:, 0, 0, P:3 * P], rs[:, 1:2], None,
                                      ALU.mult).then_inc(p_part, 1)
                    dve.wait_ge(p_part, 3 * diff + 3)
                    dve.scalar_tensor_tensor(out=p_sb[:, 0:P], in0=sc[:, 0, 1, 0:P], scalar=rs[:, 2:3],
                                             in1=p_sb[:, 0:P], op0=ALU.mult, op1=ALU.add)
                    dve.scalar_tensor_tensor(out=p_sb[:, P:3 * P], in0=sc[:, 0, 1, P:3 * P], scalar=rs[:, 3:4],
                                             in1=p_sb[:, P:3 * P], op0=ALU.mult, op1=ALU.add).then_inc(p_ready, 1)
                if old is not None and k == 4:
                    dve.wait_ge(y_hi, old + 1)
                    dve.scalar_tensor_tensor(out=Y_lo[:, old, :], in0=ps[4][:, 0:S], scalar=subln_s[:, 1:2],
                                             in1=Y_hi[:, old, :].bitcast(F32), op0=ALU.mult,
                                             op1=ALU.subtract).then_inc(y_lo, 1)
                if stick is not None and k == 6:
                    dve.wait_ge(y_hi, stick + 1)
                    dve.tensor_tensor(Y_lo[:, stick, :], ps[7][:, 0:S], Y_hi[:, stick, :].bitcast(F32),
                                      ALU.subtract).then_inc(y_lo, 1)

            def unit_ab(U, par, wd_next=WA, **heads):
                for k in range(STEPS):
                    split(U, k + RING, WA if k + RING < STEPS else wd_next)
                    if isinstance(U, int) and U == 0:
                        if k in (0, 2, 4):
                            turn_low(T_X0 + k // 2 + 1, 4 * (k // 2 + 1), (X_hi, X_lo), 0)
                        if k == 1:
                            angles()
                        if k == 7:
                            stat(0)
                    slot_ab(k, par, **heads)

            unit_ab(0, 0)
            unit_ab(1, 1, diff=0)
            unit_ab(2, 0, diff=1, old=0)
            unit_ab(3, 1, diff=2, old=1)
            with dve.Fori(2, HEADS_A // 2) as i:
                unit_ab(2 * i, 0, diff=2 * i - 1, old=2 * i - 2)
                unit_ab(2 * i + 1, 1, diff=2 * i, old=2 * i - 1)
            unit_ab(8, 0, diff=7, old=6)
            unit_ab(9, 1, old=7, stick=8, first_stick=True)
            with dve.Fori(HEADS_A + 2, HEADS - 1) as u:
                unit_ab(u, None, stick=u - 1)
            unit_ab(HEADS - 1, None, wd_next=W, stick=HEADS - 2)

            def unit_out(U, par, n, before, heads=None, low=None, low_k=3):
                for k in range(STEPS):
                    split(U, k + RING, W)
                    if heads is not None:
                        slot_ab(k, None, **heads)
                    if low is not None and k == low_k:
                        turn_low(*low)
                add(U, par, n, before)

            Xs, Ys = (X_hi, X_lo), (Y_hi, Y_lo)
            for n in range(NC):
                unit_out(U_OAB + n, n % 2, n, n, heads=dict(stick=HEADS - 1) if n == 0 else None,
                         low=(T_X1 + n - 1, 4 * (n - 1), Xs, 1) if n > 0 else None)

            def mlp(s, U0, T_in, T_h, adds, norm, first, last, very_last):
                a = adds + NC * s
                for n in range(2 * NC):
                    U, par = U0 + 2 * NC * s + n, n % 2
                    for k in range(STEPS):
                        if not (very_last and n == 2 * NC - 1 and k + RING >= STEPS):
                            split(U, k + RING, W)
                        if n == 0 and first and k == 2:
                            stat(norm)
                        if n == 0 and first and k == 3:
                            turn_low(T_in + NC - 1, 4 * (NC - 1), Xs, norm)
                        if 1 <= n <= NC and k == 4:
                            turn_low(T_h + NC * s + n - 1, 4 * (n - 1), Ys)
                        if n > NC and last and k == 3:
                            turn_low(T_h + NC * SUPER + n - NC - 1, 4 * (n - NC - 1), Xs, norm + 1)
                    if n >= NC:
                        add(U, par, n - NC, a + n - NC)

            def mlps(U0, T_in, T_h, adds, norm, final):
                mlp(0, U0, T_in, T_h, adds, norm, True, False, False)
                with dve.Fori(1, SUPER - 1) as s:
                    mlp(s, U0, T_in, T_h, adds, norm, False, False, False)
                mlp(SUPER - 1, U0, T_in, T_h, adds, norm, False, not final, final)

            mlps(U_MLP0, T_X1, T_H0, NC, 1, False)

            def maxima(g, j):
                n = PAIRS * g + j
                late = not isinstance(n, int) or n >= 2
                dve.wait_ge(c_scores, n + 1)
                if late:
                    dve.wait_ge(c_pT, n - 1)
                dve.memset(spare, 0.0)
                for e in range(2):
                    for q, r in ((0, slice(0, P)), (1, slice(P, 3 * P))):
                        c = 2 * e + q
                        last_ = dve.tensor_tensor_reduce(out=sc[:, j % 2, e, r], in0=ps[6 + e][:, r],
                                                         in1=band[:, r], scale=1.0, scalar=-3.0e38,
                                                         op0=ALU.add, op1=ALU.max,
                                                         accum_out=mx_c[j % 2][:, c:c + 1])
                last_.then_inc(c_max, 1)
                dve.wait_ge(c_max, n + 1)
                if late:
                    dve.wait_ge(c_sub, n - 1)
                sink = sink8[:, n, :]
                dve.tensor_tensor(M_c[j % 2], mx_c[j % 2], sink, ALU.max).then_inc(c_m, 1)
                dve.wait_ge(c_m, n + 1)
                if late:
                    dve.wait_ge(c_exp, n - 1)
                dve.tensor_tensor(d_c[j % 2], sink, M_c[j % 2], ALU.subtract).then_inc(c_d, 1)

            def evac_pT(g, j):
                n = PAIRS * g + j
                dve.wait_ge(c_pT, n + 1)
                if not isinstance(n, int) or n > 0:
                    dve.wait_ge(c_pv, n)
                dve.tensor_copy(pT[:, 1, :], ps[5][:, 0:3 * P]).then_inc(c_pT_v, 1)

            def normalise(g, j, bank=2):
                n = PAIRS * g + j
                dve.wait_ge(c_pv, n + 1)
                o4 = ps[bank][:, 0:4 * (DH + 1)].rearrange("p (e q c) -> p e q c", e=2, q=2)
                dve.tensor_tensor(den.rearrange("p (e q) -> p e q", e=2), o4[:, :, :, DH],
                                  es_c[j].rearrange("p (e q) -> p e q", e=2), ALU.add).then_inc(c_den, 1)
                dve.wait_ge(c_den, 2 * n + 1)
                dve.reciprocal(rden, den).then_inc(c_den, 1)
                dve.wait_ge(c_den, 2 * n + 2)
                if j == 0:
                    dve.wait_ge(turned, 2 * (T_C + g))
                on = on_sb[:, :].rearrange("p (t c) -> p t c", t=TB)[:, :, j * P:(j + 1) * P]
                dve.tensor_tensor(on.rearrange("p t (e d) -> p e t d", e=2), o4[:, :, :, 0:DH],
                                  rden.rearrange("p (e q) -> p e q", e=2)[:, :, :, None].to_broadcast([P, 2, 2, DH]),
                                  ALU.mult).then_inc(c_on, 1)

            def rope_group(k, g):
                rot_g, rot2_g = (v[:, :].rearrange("p (t c) -> p t c", t=TB) for v in (rot, rot2))
                if k == 0:
                    dve.wait_ge(proj_ready, HEADS + 2 + g)
                    dve.wait_ge(qkT_done, HEADS + g)
                    rope_x(HEADS_A + 1 + g, wide(0), rot_g, 8)
                if k == 1:
                    rope_sum(HEADS_A + 1 + g, rot_g, rot2_g)

            def win_slot(k, g, old):
                if k <= 1:
                    rope_group(k, g)
                if old is not None and k == 0:
                    evac_pT(old, 3)
                    normalise(old, 2)
                if old is not None and k == 1:
                    normalise(old, 3)
                if old is not None and k == 2:
                    turn_low(T_C + old, 4 * old, Ys)
                last_group = isinstance(g, int) and g == GROUPS - 1
                if k >= 5 and not (last_group and k > 5):
                    evac_pT(g, k - 5)
                if 3 <= k <= 6:
                    maxima(g, k - 3)
                if k >= 6 and not last_group:
                    normalise(g, k - 6)

            def unit_c(U, hooks, first=False, kv_unit=None):
                for k in range(STEPS):
                    split(U, k + RING, W)
                    if first and k == 2:
                        stat(2)
                    if first and k == 3:
                        turn_low(T_X2 + NC - 1, 4 * (NC - 1), Xs, 2)
                    if kv_unit is not None and k <= 1:
                        krot_t, rot2_t = krot[:, :, :], rot2[:, 0:TB * S].rearrange("p (t c) -> p t c", t=TB)
                        if k == 0:
                            dve.wait_ge(proj_ready, HEADS + 1)
                            rope_x(HEADS_A, kv[:, :, 0:S], krot_t, GROUPS)
                        else:
                            rope_sum(HEADS_A, krot_t, rot2_t)
                    if hooks is not None:
                        win_slot(k, *hooks)

            unit_c(U_C, None, first=True)
            unit_c(U_C + 1, None, kv_unit=True)
            unit_c(U_C + 2, (0, None))
            with dve.Fori(1, GROUPS - 1) as g:
                unit_c(U_C + 2 + g, (g, g - 1))

            added = NC + NC * SUPER
            g = GROUPS - 1
            for n in range(NC):
                U = U_OC + n
                for k in range(STEPS):
                    split(U, k + RING, W)
                    if n == 0:
                        win_slot(k, g, g - 1)
                        if k == 6:
                            evac_pT(g, 1)
                        if k == 7:
                            normalise(g, 0, 6)
                            evac_pT(g, 2)
                    if n == 1:
                        if k == 0:
                            normalise(g, 1, 6)
                            evac_pT(g, 3)
                        if k == 1:
                            normalise(g, 2, 6)
                        if k == 2:
                            normalise(g, 3, 6)
                        if k == 3:
                            turn_low(T_C + g, 4 * g, Ys)
                        if k == 6:
                            add(U, 0, 0, added, 6)
                    if n >= 2:
                        for c in ((0, 1) if n == 2 else (2,)):
                            if k == (0, 2, 2)[c]:
                                turn_low(T_X3 + c, 4 * c, Xs, 3)
                if n >= 1:
                    add(U, n % 2, n, added + n)

            mlps(U_MLP1, T_X3, T_H1, added + NC, 3, True)
            stat(4)
            dve.wait_ge(stat_ready, 5)
            dve.wait_ge(w_landed[0], 16 * U_END + 16)
            for t in range(TB):
                dve.scalar_tensor_tensor(out=x_sb[:, t, :], in0=x_sb[:, t, :], scalar=rstd[:, 4, t:t + 1],
                                         in1=final_g, op0=ALU.mult, op1=ALU.mult).then_inc(fin, 1)

        @block.gpsimd
        def _(pool):
            zeros = [ident, band, full, strict]
            fills = [(t, 0.0) for t in zeros] + [(strict01, 1.0), (neg_tri, -1.0), (neg_one, -1.0), (half_pow, -0.5)]
            for t, v in fills:
                pool.memset(t[:, :], v).then_inc(made_part, 1)
            pool.memset(v_cur[:, :, :], 1.0).then_inc(made_part, 1)
            for f in range(DH // 2):
                freq = np.float32(10000.0) ** np.float32(-2.0 * f / DH)
                pool.memset(inv_freq[:, f:f + 1], float(freq)).then_inc(made_part, 1)
            pool.wait_ge(made_part, len(fills) + 1 + DH // 2)

            def keep(view, op, fill, down, along):
                return pool.affine_select(out=view, in_=view, compare_op=op, fill=fill, base=0,
                                          pattern=[[along, P]], channel_multiplier=down)

            for b in (0, 2):
                cols = slice(b * P, (b + 1) * P)
                keep(band[:, cols], ALU.is_ge, NEG, 1, -1)
                keep(full[:, cols], ALU.is_ge, NEG, 1, -1)
                keep(strict[:, cols], ALU.is_gt, NEG, -1, 1)
            keep(band[:, P:2 * P], ALU.is_gt, NEG, -1, 1)
            keep(strict01[:, :], ALU.is_gt, 0.0, -1, 1)
            keep(neg_tri[:, :], ALU.is_ge, 0.0, 1, -1)
            keep(ident[:, :], ALU.not_equal, 1.0, 1, -1).then_inc(made, 1)

            def rsqrt(i):
                pool.wait_ge(stat_v, 2 * i + 2)
                pool.tensor_tensor(rstd[:, i, :], ms[:, i, :], half_pow[:, :], ALU.pow).then_inc(stat_ready, 1)

            def rope(n, src, tmp, groups):
                def halves(v, h):
                    return v.rearrange("p t (g h d) -> p t g h d", h=2, d=DH // 2)[:, :, :, h, :]

                def over(table):
                    return table[:, :, None, :].to_broadcast([P, TB, groups, DH // 2])

                if not isinstance(n, int) or n > 0:
                    pool.wait_ge(rope_ready, n)
                pool.tensor_tensor(halves(tmp, 0), halves(src, 1), over(nsin), ALU.mult).then_inc(rope_sin, 1)
                pool.tensor_tensor(halves(tmp, 1), halves(src, 0), over(sin), ALU.mult).then_inc(rope_sin, 1)

            def rope_head(h, par):
                pool.wait_ge(proj_ready, h + 1)
                rope(h, qkv(par)[:, :, 0:S], rot2[:, 0:TB * S].rearrange("p (t c) -> p t c", t=TB), 4)

            def rsqrt_head(h):
                pool.wait_ge(oss_ready, h + 1)
                if not isinstance(h, int) or h > 0:
                    pool.wait_ge(on_ready, h)
                pool.tensor_tensor(ors, oss, half_pow[:, :], ALU.pow).then_inc(ors_ready, 1)

            rsqrt(0)
            pool.wait_ge(trig, 1)
            rope_head(0, 0)
            rope_head(1, 1)
            rsqrt_head(0)
            with pool.Fori(1, HEADS_A // 2) as i:
                rope_head(2 * i, 0)
                rsqrt_head(2 * i - 1)
                rope_head(2 * i + 1, 1)
                rsqrt_head(2 * i)
            rsqrt_head(HEADS_A - 1)
            rsqrt(1)

            def square(k, buf):
                pool.wait_ge(relu_ready, k + 1)
                pool.tensor_tensor(proj[:, buf, :], proj[:, buf, :], proj[:, buf, :], ALU.mult).then_inc(hid_ready, 1)

            with pool.Fori(0, NC * SUPER // 2) as i:
                square(2 * i, 0)
                square(2 * i + 1, 1)
            rsqrt(2)

            pool.wait_ge(proj_ready, HEADS + 1)
            wide_t = "p (t c) -> p t c"
            rope(HEADS_A, kv[:, :, 0:S], rot2[:, 0:TB * S].rearrange(wide_t, t=TB), GROUPS)
            pool.wait_ge(rope_ready, HEADS_A + 1)

            def group(g):
                if not isinstance(g, int) or g > 0:
                    pool.wait_ge(qkT_done, HEADS + g)
                pool.tensor_copy(k_cur[:, :, :, :],
                                 krot[:, :, some(g * DH, DH)][:, :, None, :].to_broadcast([P, TB, 2, DH])
                                 ).then_inc(k_ready, 1)
                pool.wait_ge(proj_ready, HEADS + 2 + g)
                rope(HEADS_A + 1 + g, wide(0), rot2[:, :].rearrange(wide_t, t=TB), 8)
                if not isinstance(g, int) or g > 0:
                    pool.wait_ge(c_pv, PAIRS * g)
                pool.tensor_copy(v_cur[:, :, 0:DH], kv[:, :, some(g * DH + GROUPS * DH, DH)]).then_inc(v_ready, 1)

            def shift(g, j):
                n = PAIRS * g + j
                pool.wait_ge(c_m, n + 1)
                for q, r in ((0, slice(0, P)), (1, slice(P, 3 * P))):
                    v = sc[:, j % 2, :, r]
                    m = M_c[j % 2].rearrange("p (e q) -> p e q", q=2)[:, :, q:q + 1]
                    last = pool.tensor_tensor(v, v, m.to_broadcast([P, 2, r.stop - r.start]), ALU.subtract)
                last.then_inc(c_sub, 1)

            def groups(g):
                group(g)
                for j in range(PAIRS):
                    shift(g, j)

            groups(0)
            with pool.Fori(1, GROUPS) as g:
                groups(g)
            rsqrt(3)
            with pool.Fori(NC * SUPER // 2, NC * SUPER) as i:
                square(2 * i, 0)
                square(2 * i + 1, 1)
            rsqrt(4)


def kernel(x, positions, norm_mix, norm_mlp, norm_final, w_in_ab, w_out_ab,
           lambda_q1, lambda_k1, lambda_q2, lambda_k2, diff_subln,
           w_in_c, w_out_c, sinks, w_up, w_down):
    import concourse.bacc as bacc
    from concourse.bass_utils import run_bass_kernel_spmd

    c = np.ascontiguousarray

    def loads(w):
        u, _, n = w.shape
        return c(w.reshape(u, LOADS, LK, P, n).transpose(0, 1, 3, 2, 4).reshape(u * LOADS, P, LK * n))

    def by_columns(w, n):
        return w.reshape(D, -1, n).transpose(1, 0, 2)

    w_in_ab, w_in_c, positions = np.asarray(w_in_ab)[0], np.asarray(w_in_c)[0], np.asarray(positions)
    x, w_up, w_down = np.asarray(x), np.asarray(w_up), np.asarray(w_down)
    ab = w_in_ab.reshape(D, 2, 3, HEADS_A, P).transpose(1, 3, 0, 2, 4).reshape(HEADS, D, WA)
    cw = np.concatenate([w_in_c[:, D:], w_in_c[:, :D]], axis=1)
    up = w_up.reshape(2, D, SUPER, NC, W).transpose(0, 2, 3, 1, 4)
    down = w_down.reshape(2, SUPER, D, NC, W).transpose(0, 1, 3, 2, 4)
    mlp = np.concatenate([up, down], axis=2).reshape(-1, D, W)
    norms = np.stack([norm_mix[0], norm_mlp[0], norm_mix[1], norm_mlp[1]])
    oc = loads(by_columns(np.asarray(w_out_c)[0], W))
    oc = np.concatenate([oc[[LOADS * n + j for n, j in PAIR_ORDER]], oc[2 * LOADS:]])
    arrays = {
        "x": c(x[0]),
        "positions": c(positions[0].reshape(TB, P).T),
        "norm_t": c(norms.reshape(4, KT, P).transpose(2, 0, 1)),
        "norm_final": c(np.broadcast_to(np.asarray(norm_final), (P, D))),
        "w_ab": loads(ab),
        "w_oab": loads(by_columns(np.asarray(w_out_ab)[0], W)),
        "w_mlp": loads(mlp),
        "w_c": loads(by_columns(cw, W)),
        "w_oc": oc,
        "lambdas": c(np.broadcast_to(np.concatenate([np.asarray(v)[0] for v in
                                                     (lambda_q1, lambda_k1, lambda_q2, lambda_k2)]), (P, 4 * DH))),
        "subln": c(np.asarray(diff_subln)[0].reshape(P, 1)),
        "sinks": c(np.broadcast_to(np.asarray(sinks)[0], (P, 2 * GROUPS * PAIRS))),
    }
    nc = bacc.Bacc("TRN2", target_bir_lowering=False, num_devices=1)
    args = [nc.dram_tensor(f"in_{n}", a.shape, mybir.dt.from_np(a.dtype), kind="ExternalInput").ap()
            for n, a in arrays.items()]
    args.append(nc.dram_tensor("out", (S, D), F32, kind="ExternalOutput").ap())
    trunk_kernel(nc, *args)
    r = run_bass_kernel_spmd(nc, [{f"in_{n}": a for n, a in arrays.items()}], core_ids=[0])
    return r.results[0]["out"].reshape(1, S, D)
```
